# Optimizing a Trainium2 kernel written in Bass

```python
import jax, jax.numpy as jnp
from jax import lax
import numpy as np

D_MODEL = 1024
BATCH = 1
SEQ = 1024
DEPTH = 1

HEAD_DIM = 64
N_SB_HEADS = 8
N_FOX_HEADS = 8
D_SB = N_SB_HEADS * HEAD_DIM
D_FOX = N_FOX_HEADS * HEAD_DIM
D_MIX = D_SB + D_FOX
D_IN = 3 * D_SB + 3 * D_FOX + D_MIX + N_FOX_HEADS
Q_BLOCK = 128
EPS = 1e-6

kernel_name = "hybrid_stickbreaking_fox_adaln"

def rmsnorm(x, g):
    x32 = x.astype(jnp.float32)
    r = lax.rsqrt(jnp.mean(x32 * x32, axis=-1, keepdims=True) + EPS)
    return (x32 * r).astype(x.dtype) * g

def to_heads(t, n_heads):
    b, s, _ = t.shape
    return t.reshape(b, s, n_heads, HEAD_DIM).transpose(0, 2, 1, 3)

def from_heads(t):
    b, h, s, d = t.shape
    return t.transpose(0, 2, 1, 3).reshape(b, s, h * d)

def to_query_blocks(t):
    b, h, s = t.shape[:3]
    nb = s // Q_BLOCK
    t = t.reshape((b, h, nb, Q_BLOCK) + t.shape[3:])
    return jnp.moveaxis(t, 2, 0)

def from_query_blocks(t):
    nb, b, h, qb, d = t.shape
    return jnp.moveaxis(t, 0, 2).reshape(b, h, nb * qb, d)

def stick_breaking_attention(q, k, v):
    s_len = q.shape[2]
    scale = HEAD_DIM ** -0.5
    key_pos = jnp.arange(s_len)

    def block(args):
        qb, i = args
        q_pos = i * Q_BLOCK + jnp.arange(Q_BLOCK)
        z = jnp.einsum('bhqd,bhkd->bhqk', qb, k).astype(jnp.float32) * scale
        causal = key_pos[None, :] < q_pos[:, None]
        log_rem = jnp.where(causal, jax.nn.log_sigmoid(-z), 0.0)
        after = lax.cumsum(log_rem, axis=3, reverse=True) - log_rem
        a = jnp.where(causal, jnp.exp(jax.nn.log_sigmoid(z) + after), 0.0)
        return jnp.einsum('bhqk,bhkd->bhqd', a.astype(v.dtype), v)

    out = lax.map(block, (to_query_blocks(q), jnp.arange(s_len // Q_BLOCK)))
    return from_query_blocks(out)

def forgetting_attention(q, k, v, log_f):
    s_len = q.shape[2]
    scale = HEAD_DIM ** -0.5
    key_pos = jnp.arange(s_len)
    cum = lax.cumsum(log_f, axis=2)

    def block(args):
        qb, cum_q, i = args
        q_pos = i * Q_BLOCK + jnp.arange(Q_BLOCK)
        logits = jnp.einsum('bhqd,bhkd->bhqk', qb, k).astype(jnp.float32) * scale
        logits = logits + cum_q[..., :, None] - cum[..., None, :]
        causal = key_pos[None, :] <= q_pos[:, None]
        p = jax.nn.softmax(jnp.where(causal, logits, -jnp.inf), axis=-1)
        return jnp.einsum('bhqk,bhkd->bhqd', p.astype(v.dtype), v)

    out = lax.map(block, (to_query_blocks(q), to_query_blocks(cum), jnp.arange(s_len // Q_BLOCK)))
    return from_query_blocks(out)

def setup_inputs(seed: int = 0) -> dict:
    key = jax.random.key(seed)
    ks = jax.random.split(key, 12)
    x = jax.random.normal(ks[0], (BATCH, SEQ, D_MODEL), jnp.float32)
    c = jax.random.normal(ks[1], (BATCH, D_MODEL), jnp.float32)
    w_ada = jax.random.normal(ks[2], (DEPTH, D_MODEL, 3 * D_MODEL), jnp.float32) * (0.1 * D_MODEL ** -0.5)
    b_ada = jax.random.normal(ks[3], (DEPTH, 3 * D_MODEL), jnp.float32) * 0.02
    g_norm = 1.0 + 0.02 * jax.random.normal(ks[4], (DEPTH, D_MODEL), jnp.float32)
    w_in = jax.random.normal(ks[5], (DEPTH, D_MODEL, D_IN), jnp.float32) * (D_MODEL ** -0.5)
    b_f = (jnp.linspace(1.0, 6.0, N_FOX_HEADS, dtype=jnp.float32)[None, :]
           + 0.1 * jax.random.normal(ks[6], (DEPTH, N_FOX_HEADS), jnp.float32))
    g_grp = 1.0 + 0.02 * jax.random.normal(ks[7], (DEPTH, D_MIX), jnp.float32)
    w_out = jax.random.normal(ks[8], (DEPTH, D_MIX, D_MODEL), jnp.float32) * (D_MIX ** -0.5)
    g_final = 1.0 + 0.02 * jax.random.normal(ks[9], (D_MODEL,), jnp.float32)
    return {"x": x, "c": c, "w_ada": w_ada, "b_ada": b_ada, "g_norm": g_norm,
            "w_in": w_in, "b_f": b_f, "g_grp": g_grp, "w_out": w_out, "g_final": g_final}

def reference(x, c, w_ada, b_ada, g_norm, w_in, b_f, g_grp, w_out, g_final):
    split_points = list(np.cumsum([D_SB, D_SB, D_SB, D_FOX, D_FOX, D_FOX, D_MIX]))
    c_act = jax.nn.silu(c)
    for layer in range(DEPTH):
        ada = c_act @ w_ada[layer] + b_ada[layer]
        shift, scale, gate = jnp.split(ada, 3, axis=-1)
        h = rmsnorm(x, g_norm[layer]) * (1.0 + scale[:, None, :]) + shift[:, None, :]

        z = h @ w_in[layer]
        q_sb, k_sb, v_sb, q_fx, k_fx, v_fx, g_path, f_logit = jnp.split(z, split_points, axis=-1)

        o_sb = from_heads(stick_breaking_attention(
            to_heads(q_sb, N_SB_HEADS), to_heads(k_sb, N_SB_HEADS), to_heads(v_sb, N_SB_HEADS)))

        log_f = jax.nn.log_sigmoid((f_logit + b_f[layer]).astype(jnp.float32)).transpose(0, 2, 1)
        o_fx = from_heads(forgetting_attention(
            to_heads(q_fx, N_FOX_HEADS), to_heads(k_fx, N_FOX_HEADS), to_heads(v_fx, N_FOX_HEADS), log_f))

        y = jnp.concatenate([rmsnorm(o_sb, g_grp[layer, :D_SB]),
                             rmsnorm(o_fx, g_grp[layer, D_SB:])], axis=-1)
        y = y * jax.nn.silu(g_path)
        x = x + (1.0 + gate[:, None, :]) * (y @ w_out[layer])
    return rmsnorm(x, g_final)


_drawn_inputs = setup_inputs


def setup_inputs(seed=0):
    import zlib

    import numpy as np

    out = dict(_drawn_inputs(seed))
    spreads = {}
    factors = {'g_norm': 3.303, 'g_grp': 5.587, 'g_final': 2.848}
    for name, (base, spread) in spreads.items():
        noise = np.random.default_rng([zlib.crc32(name.encode()), seed]).standard_normal(out[name].shape)
        drawn = base * np.exp(spread * noise) if base else spread * noise
        out[name] = __import__('jax').numpy.asarray(drawn.astype(out[name].dtype))
    for name, factor in factors.items():
        out[name] = (out[name] * factor).astype(out[name].dtype)
    return out
```

```python
from contextlib import ExitStack

import numpy as np

import concourse.bass as bass
from concourse import mybir


def hybrid_trunk_kernel(nc, x, c, w_ada_t, b_ada_cols, g_norm_cols, w_in, b_f_col, g_grp_cols, w_out, g_final,
                        identity, out):
    fp32 = mybir.dt.float32
    fp32r = mybir.dt.float32r
    bf16 = mybir.dt.bfloat16
    ALU = mybir.AluOpType
    ACT = mybir.ActivationFunctionType

    P = 128
    SEQ, D = x.shape
    HD = 64
    DC = D // P
    TB = SEQ // P
    HALF = 512
    NHALF = SEQ // HALF
    N_TYPE = 512
    PAIRS = 2 * N_TYPE // P
    STEPS = 2 * TB
    UNITS = PAIRS * STEPS
    GROUPS = UNITS // 2
    EPS = 1e-6
    MASKED = -1e30
    SCALE = HD ** -0.5
    LOWEST = -3e38

    def is_sb(g):
        return (g // STEPS) % 2 == 0

    def unit(g):
        return g // STEPS, (g % STEPS) // TB, g % TB

    def pieces(g):
        n = (g % TB + 1) * P
        return [(a, min(a + HALF, n)) for a in range(0, n, HALF)]

    def tgroups(g):
        n = g % TB + 1
        return [(a, min(a + 4, n)) for a in range(0, n, 4)]

    def numbered(events):
        return {e: i + 1 for i, e in enumerate(events)}

    blocks = [(0, "q"), (0, "k"), (0, "v"), (-1, "f")]
    for p in range(PAIRS):
        if p + 1 < PAIRS:
            blocks += [(p + 1, "q"), (p + 1, "k"), (p, "g"), (p + 1, "v")]
        else:
            blocks += [(p, "g")]
    N_FIRST = 4
    units = [(p, kind, h) for p, kind in blocks for h in range(NHALF)]
    block_no = {b: i for i, b in enumerate(blocks)}
    unit_no = {u: i for i, u in enumerate(units)}

    def w_columns(p, kind):
        t, j = p % 2, p // 2
        if kind == "f":
            return w_in[:, 8 * N_TYPE:8 * N_TYPE + 8], 8
        base = 6 * N_TYPE + t * N_TYPE if kind == "g" else (3 * t + "qkv".index(kind)) * N_TYPE
        return w_in[:, base + P * j:base + P * (j + 1)], P

    all_units = list(range(UNITS))
    S_PIECE = numbered([(g, j) for g in all_units for j in range(len(pieces(g)))])
    SB_PIECE = numbered([(g, j) for g in all_units if is_sb(g) for j in range(len(pieces(g)))])
    FX_PIECE = numbered([(g, j) for g in all_units if not is_sb(g) for j in range(len(pieces(g)))])
    SB_UNIT = numbered([g for g in all_units if is_sb(g)])
    FX_UNIT = numbered([g for g in all_units if not is_sb(g)])
    piece_list = list(S_PIECE)

    t_items = []
    for g in all_units + [UNITS]:
        p, i = g // STEPS, g % STEPS
        if g < UNITS and i == 0:
            t_items += [("V", p, 0), ("V", p, 1)]
        if p >= 1 and i == (4 if g < UNITS else 0) or g == UNITS:
            t_items.append(("SS", p - 1, 0))
        if g < UNITS:
            t_items += [("T", g, j) for j in range(len(tgroups(g)))]
    T_ITEM = numbered(t_items)
    T_HI = numbered([e for e in t_items if e[0] != "SS"])
    LO_UNITS = numbered([u for u in units if u[1] != "v"])

    x_tiles = x.rearrange("(t p) d -> t p d", p=P)
    out_tiles = out.rearrange("(t p) d -> t p d", p=P)
    ada_tiles = w_ada_t.rearrange("(n p) k -> n p k", p=P)
    N_ADA = ada_tiles.shape[0]
    wo_tiles = w_out.rearrange("(m p) n -> m p n", p=P)

    ctx = ExitStack()
    with ctx:
        def sb(name, shape, dt=fp32):
            return ctx.enter_context(nc.sbuf_tensor(name, shape, dt))

        def sem(name):
            return ctx.enter_context(nc.semaphore(name))

        y_dram = nc.dram_tensor("y_scratch", (PAIRS, P, SEQ), fp32, kind="Internal").ap()
        c_dram = nc.dram_tensor("forget_scratch", (8, SEQ), fp32, kind="Internal").ap()
        gate_dram = nc.dram_tensor("gate_scratch", (1, D), fp32, kind="Internal").ap()

        h_hi = sb("h_hi", [P, DC, SEQ], fp32r)
        h_lo = sb("h_lo", [P, DC, SEQ], fp32r)
        w_raw = sb("w_raw", [P, DC, P])
        w_hi = sb("w_hi", [P, 2, DC, P], fp32r)
        w_lo = sb("w_lo", [P, 2, DC, P], fp32r)
        stacks = sb("stacks", [P, 2, 2, 3, SEQ], fp32r)
        v_stack = sb("v_stack", [P, 2, 2, TB, P], fp32r)
        pt_hi = sb("pt_hi", [P, TB, 2 * P], fp32r)
        pt_lo = sb("pt_lo", [P, TB, 2 * P], fp32r)
        work = sb("work", [P, 9, SEQ])
        U = [work[:, 0, :], work[:, 1, :]]
        R = [work[:, 2, :], work[:, 3, :]]
        CUM = [work[:, 4, :], work[:, 5, :]]
        VT = work[:, 6, :]
        O_T = work[:, 7, :]
        G_T = work[:, 8, :]
        o_shift = sb("o_shift", [P, 2, 2 * P])
        ident = sb("ident", [P, P])
        ident_bf = sb("ident_bf", [P, P], bf16)
        mask_f = sb("mask_f", [P, 2, P])
        mask_bf = sb("mask_bf", [P, 2, P], bf16)
        ones = sb("ones", [P, 1])
        small = sb("small", [P, 192])
        ada = small[:, 0:24]
        b_ada_sb = small[:, 24:48]
        g_norm_sb = small[:, 48:56]
        g_grp_sb = small[:, 56:64]
        a_cols = small[:, 64:72]
        ss_x = small[:, 72:80]
        rms_v = small[:, 80:96]
        rms_s = small[:, 96:112]
        rms_y = small[:, 112:128]
        rms_t = small[:, 128:144]
        ss_o = small[:, 144:160]
        b_f_sb = small[0:8, 160:161]
        row_max = small[:, 164:168]
        neg_max = small[:, 168:170]
        row_sum = small[:, 170:172]
        row_inv = small[:, 172:174]
        bf_neg = small[0:8, 174:175]

        psum = ctx.enter_context(nc.psum_tensor("psum", [P, 8, 512], fp32))
        PROJ = [psum[:, 0, :], psum[:, 1, :]]
        SCORE = [psum[:, 2, :], psum[:, 3, :], psum[:, 4, :]]
        TRANS = [psum[:, 5, :], psum[:, 6, :]]
        OUT = psum[:, 7, :]

        s_const = sem("s_const")
        s_x = [sem(f"s_x{i}") for i in range(4)]
        s_wa = [sem(f"s_wa{i}") for i in range(4)]
        s_c = sem("s_c")
        s_csig = sem("s_csig")
        s_cact = sem("s_cact")
        s_ada = sem("s_ada")
        s_acol = sem("s_acol")
        s_ssx = sem("s_ssx")
        s_rv = sem("s_rv")
        s_rs = sem("s_rs")
        s_rn = sem("s_rn")
        s_xn = sem("s_xn")
        s_xt = sem("s_xt")
        s_hhi = sem("s_hhi")
        s_hf = sem("s_hf")
        s_hlo = sem("s_hlo")
        s_mask = sem("s_mask")
        s_maskb = sem("s_maskb")
        s_ones = sem("s_ones")
        s_wraw = sem("s_wraw")
        s_whi = sem("s_whi")
        s_wlo = sem("s_wlo")
        s_proj = sem("s_proj")
        s_phi = sem("s_phi")
        s_plo = sem("s_plo")
        s_f = sem("s_f")
        s_fa = sem("s_fa")
        s_cum = sem("s_cum")
        s_cumb = sem("s_cumb")
        s_score = sem("s_score")
        s_sig = sem("s_sig")
        s_scan = sem("s_scan")
        s_logit = sem("s_logit")
        s_max = sem("s_max")
        s_exp = sem("s_exp")
        s_inv = sem("s_inv")
        s_prob = sem("s_prob")
        s_t = sem("s_t")
        s_thi = sem("s_thi")
        s_tfree = sem("s_tfree")
        s_pv = sem("s_pv")
        s_pvs = sem("s_pvs")
        s_pvd = sem("s_pvd")
        s_y = sem("s_y")
        s_sq = sem("s_sq")
        s_yst = sem("s_yst")
        s_yld = [sem(f"s_yld{i}") for i in range(4)]
        s_yhi = sem("s_yhi")
        s_ylo = sem("s_ylo")
        s_gate = sem("s_gate")
        s_gst = sem("s_gst")
        s_row = sem("s_row")
        s_op = sem("s_op")
        s_osb = sem("s_osb")
        s_ofx = sem("s_ofx")
        s_fin = sem("s_fin")
        s_fsq = sem("s_fsq")
        s_done = sem("s_done")
        s_xr = [sem(f"s_xr{i}") for i in range(2)]
        s_store = [sem(f"s_store{i}") for i in range(2)]

        block = ctx.enter_context(nc.Block())

        XBANK = [0, 1, 2, 3, 4, 5, 6, 7]

        def x_piece_bank(n):
            return XBANK[n] if n < 8 else XBANK[2 + (n - 8) % 6]

        def w_slot(b):
            return b % 2

        def y_parts(m):
            t, j = m % 2, m // 2
            flat = stacks[:, t, :, :, :].rearrange("p h s n -> p (h s) n")
            if j < 3:
                return flat[:, 2 * j, :], flat[:, 2 * j + 1, :]
            vflat = v_stack[:, t, :, :, :].rearrange("p h b n -> p h (b n)")
            return vflat[:, 0, :], vflat[:, 1, :]

        @block.sync
        def _(sp):
            sp.dma_start(ident[:], identity).then_inc(s_const, 16)
            for t in range(4):
                sp.dma_start(R[t - 2] if t >= 2 else U[t], x_tiles[t]).then_inc(s_x[t], 16)
            sp.dma_start(CUM[0], c[0:1, :].partition_broadcast(P)).then_inc(s_c, 16)
            sp.dma_start(b_ada_sb, b_ada_cols).then_inc(s_const, 16)
            sp.dma_start(g_norm_sb, g_norm_cols).then_inc(s_const, 16)
            sp.dma_start(g_grp_sb, g_grp_cols).then_inc(s_const, 16)
            sp.dma_start(b_f_sb, b_f_col).then_inc(s_const, 16)
            for n in range(2 * DC):
                if n >= 3:
                    sp.wait_ge(s_ada, n - 2)
                sp.dma_start(work[:, 6 + n % 3, :], ada_tiles[n]).then_inc(s_wa[n % 3], 16)
                if n >= 2 * DC - 4:
                    t = n - (2 * DC - 4)
                    sp.wait_ge(s_xt, DC)
                    sp.dma_start(work[:, t, :], x_tiles[4 + t]).then_inc(s_x[t], 16)

            def load_w(b):
                p, kind = blocks[b]
                src, n = w_columns(p, kind)
                if b >= 1:
                    sp.wait_ge(s_wlo, b)
                sp.dma_start(w_raw[:, :, 0:n], src.rearrange("(c p) n -> p c n", p=P)).then_inc(s_wraw, 16)

            def load_wo(m):
                sp.wait_ge(s_wlo, len(blocks) + m)
                sp.dma_start(w_raw[:].rearrange("p c n -> p (c n)"), wo_tiles[m]).then_inc(s_wraw, 16)

            for b in range(N_FIRST):
                load_w(b)
            sp.wait_ge(s_f, 4)
            sp.dma_start(c_dram, CUM[0][0:8, :]).then_inc(s_cum, 16)
            load_w(N_FIRST)
            for g in range(UNITS):
                p, i = g // STEPS, g % STEPS
                b = N_FIRST + 4 * p + i // 4 + 1
                if i % 4 == 0 and b < len(blocks):
                    load_w(b)
                if p == PAIRS - 1 and i % 2 == 0 and 4 <= i:
                    load_wo(i // 2 - 2)
                if i == 2 and p >= 1:
                    sp.wait_ge(s_y, p)
                    sp.dma_start(y_dram[p - 1], G_T).then_inc(s_yst, 16)
                if i == 3 and p % 2 == 0:
                    sp.wait_ge(s_cum, 16)
                    if p >= 2:
                        sp.wait_ge(s_logit, FX_PIECE[p * STEPS - 1, 1])
                    for a in range(2):
                        sp.dma_start(CUM[a], c_dram[p + a:p + a + 1, :].partition_broadcast(P)).then_inc(s_cumb, 16)
            for m in range(6, DC):
                load_wo(m)
            sp.wait_ge(s_y, PAIRS)
            sp.dma_start(y_dram[PAIRS - 1], G_T).then_inc(s_yst, 16)
            sp.wait_ge(s_logit, FX_PIECE[UNITS - 1, 1])
            sp.dma_start(CUM[1], c[0:1, :].partition_broadcast(P)).then_inc(s_c, 16)
            sp.wait_ge(s_t, T_ITEM["T", UNITS - 1, 1])
            sp.wait_ge(s_yst, 16 * PAIRS)
            for n in range(DC):
                if n >= 2:
                    sp.wait_ge(s_ada, 2 * DC + n - 1)
                sp.dma_start(U[n % 2], ada_tiles[2 * DC + n]).then_inc(s_wa[n % 2], 16)
                if n >= 2:
                    sp.wait_ge(s_ylo, n - 1)
                sp.dma_start(R[n % 2], y_dram[n]).then_inc(s_yld[n % 2], 16)
            sp.wait_ge(s_gate, 1)
            sp.dma_start(gate_dram.rearrange("a (b p) -> p (a b)", p=P), a_cols,
                         allow_slow_non_contiguous=True).then_inc(s_gst, 16)
            sp.wait_ge(s_gst, 16)
            sp.dma_start(CUM[0], gate_dram[0:1, :].partition_broadcast(P)).then_inc(s_row, 16)
            sp.dma_start(CUM[1], g_final[0:1, :].partition_broadcast(P)).then_inc(s_row, 16)
            for t in range(TB):
                if t == 0:
                    sp.wait_ge(s_tfree, T_ITEM["SS", PAIRS - 1, 0])
                if t >= 2:
                    sp.wait_ge(s_fin, 2 * (t - 1))
                sp.dma_start(work[:, 6 + t % 2, :], x_tiles[t]).then_inc(s_xr[t % 2], 16)
                if t >= 1:
                    sp.wait_ge(s_done, t)
                    sp.dma_start(out_tiles[t - 1], R[(t - 1) % 2]).then_inc(s_store[(t - 1) % 2], 16)
            sp.wait_ge(s_done, TB)
            sp.dma_start(out_tiles[TB - 1], R[(TB - 1) % 2]).then_inc(s_store[(TB - 1) % 2], 16)
            for slot in range(2):
                sp.wait_ge(s_store[slot], 16 * TB // 2)

        @block.gpsimd
        def _(pool):
            nc.gpsimd.memset(mask_f[:], 0.0).then_inc(s_mask, 1)
            pool.wait_ge(s_mask, 1)
            nc.gpsimd.affine_select(out=mask_f[:, 0, :], in_=mask_f[:, 0, :], compare_op=ALU.is_gt, fill=MASKED,
                                    base=0, pattern=[[-1, P]], channel_multiplier=1).then_inc(s_mask, 1)
            nc.gpsimd.affine_select(out=mask_f[:, 1, :], in_=mask_f[:, 1, :], compare_op=ALU.is_ge, fill=MASKED,
                                    base=0, pattern=[[-1, P]], channel_multiplier=1).then_inc(s_mask, 1)

            def split_w(b):
                if b >= 2:
                    pool.wait_ge(s_proj, unit_no[blocks[b - 2] + (1,)] + 1)
                pool.wait_ge(s_wraw, 16 * (b + 1))
                nc.gpsimd.tensor_scalar(w_hi[:, w_slot(b)], w_raw[:], 1.0, 1.0, ALU.mult, ALU.mult).then_inc(s_whi, 1)
                pool.wait_ge(s_whi, b + 1)
                nc.gpsimd.tensor_tensor(w_lo[:, w_slot(b)], w_raw[:], w_hi[:, w_slot(b)].bitcast(fp32),
                                        ALU.subtract).then_inc(s_wlo, 1)

            def split_wo(m):
                n = len(blocks) + m
                if m == 0:
                    pool.wait_ge(s_proj, len(units))
                pool.wait_ge(s_wraw, 16 * (n + 1))
                raw = w_raw[:].rearrange("p c n -> p (c n)")
                nc.gpsimd.tensor_scalar(h_hi[:, m, :], raw, 1.0, 1.0, ALU.mult, ALU.mult).then_inc(s_whi, 1)
                pool.wait_ge(s_whi, n + 1)
                nc.gpsimd.tensor_tensor(h_lo[:, m, :], raw, h_hi[:, m, :].bitcast(fp32),
                                        ALU.subtract).then_inc(s_wlo, 1)

            split_w(0)
            split_w(1)
            for n in range(2 * DC):
                pool.wait_ge(s_hf, n + 1)
                th, d = n // DC, n % DC
                cols = slice(th * HALF, (th + 1) * HALF)
                nc.gpsimd.tensor_tensor(h_lo[:, d, cols], CUM[1][:, (n % 2) * HALF:(n % 2 + 1) * HALF],
                                        h_hi[:, d, cols].bitcast(fp32), ALU.subtract).then_inc(s_hlo, 1)
            split_w(2)
            split_w(3)

            def sb_probs(g):
                n = (g % TB + 1) * P
                pool.wait_ge(s_scan, SB_UNIT[g])
                nc.gpsimd.tensor_tensor(U[g % 2][:, 0:n - 1], U[g % 2][:, 0:n - 1], R[g % 2][:, 1:n],
                                        ALU.mult).then_inc(s_prob, 1)

            def fx_probs(g):
                n = (g % TB + 1) * P
                pool.wait_ge(s_inv, FX_UNIT[g])
                nc.gpsimd.tensor_scalar(U[g % 2][:, 0:n], U[g % 2][:, 0:n], row_inv[:, g % 2:g % 2 + 1], 1.0,
                                        ALU.mult, ALU.mult).then_inc(s_prob, 1)

            def finish_pair(p):
                pool.wait_ge(s_pvd, (p + 1) * STEPS // 2)
                pool.wait_ge(s_plo, LO_UNITS[p, "g", 1])
                nc.gpsimd.tensor_tensor(G_T, G_T, O_T, ALU.mult).then_inc(s_y, 1)
                if p + 1 < PAIRS:
                    pool.wait_ge(s_t, T_ITEM["V", p + 1, 1])
                nc.gpsimd.tensor_tensor(VT, O_T, O_T, ALU.mult).then_inc(s_sq, 1)

            sb_probs(0)
            sb_probs(1)
            split_w(N_FIRST)
            for g in range(UNITS):
                p, i = g // STEPS, g % STEPS
                if i == 0 and p >= 1:
                    finish_pair(p - 1)
                if g + 1 < UNITS and not is_sb(g + 1):
                    fx_probs(g + 1)
                if g + 2 < UNITS and is_sb(g + 2):
                    sb_probs(g + 2)
                b = N_FIRST + 4 * p + i // 4 + 1
                if i % 4 == 0 and b < len(blocks):
                    split_w(b)
                if p == PAIRS - 1 and i % 2 == 0 and 4 <= i:
                    split_wo(i // 2 - 2)
            for m in range(6, DC):
                split_wo(m)
            finish_pair(PAIRS - 1)

        @block.scalar
        def _(act):
            act.wait_ge(s_c, 16)
            nc.scalar.activation(CUM[1], CUM[0], ACT.Sigmoid).then_inc(s_csig, 1)
            for t in range(TB):
                act.wait_ge(s_x[t % 4], 16 * (t // 4 + 1))
                nc.scalar.activation(h_hi[:, t, :], work[:, t % 4, :], ACT.Square,
                                     accum_out=ss_x[:, t:t + 1]).then_inc(s_ssx, 1)
                if t == 3 or t == TB - 1:
                    act.wait_ge(s_rv, t // 4 + 1)
                    c0 = t - 3
                    nc.scalar.activation(rms_s[:, c0:c0 + 4], rms_v[:, c0:c0 + 4], ACT.Sqrt).then_inc(s_rs, 1)
                if t == 3:
                    act.wait_ge(s_ssx, 4)
                    act.wait_ge(s_acol, 3)

            def h_piece(n):
                th, d = n // DC, n % DC
                act.wait_ge(s_xt, n + 1)
                nc.scalar.activation(h_hi[:, d, th * HALF:(th + 1) * HALF], psum[:, x_piece_bank(n), :],
                                     ACT.Identity, scale=a_cols[:, d:d + 1],
                                     bias=ada[:, d:d + 1]).then_inc(s_hhi, 1)

            act.wait_ge(s_ssx, TB)
            for n in range(2 * DC):
                h_piece(n)

            def proj_out(u):
                p, kind, th = units[u]
                bank = PROJ[u % 2]
                st = p % 2
                cols = slice(th * HALF, (th + 1) * HALF)
                act.wait_ge(s_proj, u + 1)
                if kind == "q":
                    nc.scalar.activation(stacks[0:HD, st, 0, 0, cols], bank[0:HD, :], ACT.Copy, scale=SCALE)
                    nc.scalar.activation(stacks[0:HD, st, 1, 0, cols], bank[HD:P, :], ACT.Copy,
                                         scale=SCALE).then_inc(s_phi, 1)
                elif kind == "k":
                    for a in range(2):
                        src = bank[a * HD:(a + 1) * HD, :]
                        nc.scalar.activation(stacks[0:HD, st, a, 1, cols], src, ACT.Copy)
                        last = nc.scalar.activation(stacks[HD:P, st, a, 1, cols], src, ACT.Copy)
                    last.then_inc(s_phi, 1)
                elif kind == "v":
                    if p >= 2:
                        act.wait_ge(s_tfree, T_ITEM["SS", p - 2, 0])
                    nc.scalar.activation(VT[:, cols], bank, ACT.Copy).then_inc(s_phi, 1)
                elif kind == "g":
                    if p >= 1:
                        act.wait_ge(s_yst, 16 * p)
                    nc.scalar.activation(G_T[:, cols], bank, ACT.Sigmoid).then_inc(s_phi, 1)
                else:
                    nc.scalar.activation(CUM[1][0:8, cols], bank[0:8, :], ACT.Abs, bias=b_f_sb).then_inc(s_phi, 1)

            def scores_out(g):
                for j, (a, e) in enumerate(pieces(g)):
                    if is_sb(g):
                        if j == 0 and g >= 2:
                            act.wait_ge(s_t, T_ITEM["T", g - 2, len(tgroups(g - 2)) - 1])
                        act.wait_ge(s_score, S_PIECE[g, j])
                        bank = SCORE[(S_PIECE[g, j] - 1) % 3][:, 0:e - a]
                        nc.scalar.activation(U[g % 2][:, a:e], bank, ACT.Sigmoid)
                        nc.scalar.activation(R[g % 2][:, a:e], bank, ACT.Sigmoid, scale=-1.0).then_inc(s_sig, 1)
                if not is_sb(g):
                    n = (g % TB + 1) * P
                    act.wait_ge(s_max, FX_UNIT[g])
                    nc.scalar.activation(U[g % 2][:, 0:n], U[g % 2][:, 0:n], ACT.Exp, bias=neg_max[:, g % 2:g % 2 + 1],
                                         accum_out=row_sum[:, g % 2:g % 2 + 1]).then_inc(s_exp, 1)

            def values_out(q):
                a = (q // (TB // 2)) % 2
                act.wait_ge(s_pv, q + 1)
                if q >= 2:
                    act.wait_ge(s_pvd, q - 1)
                nc.scalar.activation(o_shift[a * HD:(a + 1) * HD, q % 2, :], OUT[HD:P, 0:2 * P],
                                     ACT.Copy).then_inc(s_pvs, 1)

            def vt_out(p):
                for j in range(2):
                    n = T_ITEM["V", p, j]
                    act.wait_ge(s_t, n)
                    bank = TRANS[(n - 1) % 2].rearrange("p (b d) -> p b d", d=P)
                    for a in range(2):
                        last = nc.scalar.activation(v_stack[:, p % 2, a, 4 * j:4 * j + 4, 0:HD],
                                                    bank[:, :, a * HD:(a + 1) * HD], ACT.Copy)
                    last.then_inc(s_thi, 1)

            def pt_out(g):
                for j, (a, e) in enumerate(tgroups(g)):
                    n = T_ITEM["T", g, j]
                    act.wait_ge(s_t, n)
                    if j == 0 and g % 2 == 0 and g >= 2:
                        act.wait_ge(s_pv, g // 2)
                    bank = TRANS[(n - 1) % 2][:, 0:(e - a) * P].rearrange("p (b q) -> p b q", q=P)
                    nc.scalar.activation(pt_hi[:, a:e, (g % 2) * P:(g % 2 + 1) * P], bank,
                                         ACT.Copy).then_inc(s_thi, 1)

            def final_square(t):
                act.wait_ge(s_fin, 2 * (t + 1))
                nc.scalar.activation(U[t % 2], R[t % 2], ACT.Square, accum_out=ss_x[:, t:t + 1]).then_inc(s_fsq, 1)
                act.wait_ge(s_rv, 4 + t)
                nc.scalar.activation(row_sum[:, t % 2:t % 2 + 1], row_max[:, t % 2:t % 2 + 1], ACT.Sqrt).then_inc(s_rs, 1)

            for u in range(2 * N_FIRST):
                proj_out(u)
            act.wait_ge(s_phi, 2 * N_FIRST)
            nc.scalar.activation(CUM[1][0:8, :], CUM[1][0:8, :], ACT.Exp, scale=-1.0).then_inc(s_fa, 1)
            act.wait_ge(s_fa, 1)
            nc.scalar.activation(CUM[1][0:8, :], CUM[1][0:8, :], ACT.Ln, bias=1.0).then_inc(s_fa, 1)
            scores_out(0)
            scores_out(1)
            for g in range(UNITS):
                p, i = g // STEPS, g % STEPS
                u = 2 * N_FIRST + 8 * p + i // 2
                if i % 2 == 1 and u < len(units):
                    proj_out(u)
                if g % 2 == 0 and g >= 2:
                    values_out(g // 2 - 1)
                if i == 0:
                    vt_out(p)
                pt_out(g)
                if g + 2 < UNITS:
                    scores_out(g + 2)
            values_out(GROUPS - 1)
            act.wait_ge(s_c, 32)
            nc.scalar.activation(CUM[0], CUM[1], ACT.Sigmoid).then_inc(s_csig, 1)
            act.wait_ge(s_rv, 3)
            nc.scalar.activation(rms_s[:], rms_v[:], ACT.Sqrt).then_inc(s_rs, 1)
            act.wait_ge(s_rn, 3 * 5)
            for t in range(TB):
                act.wait_ge(s_op, t + 1)
                if t >= 2:
                    act.wait_ge(s_ofx, t - 1)
                if t == 0:
                    act.wait_ge(s_ada, 3 * DC)
                nc.scalar.activation(U[t % 2].rearrange("p (a n) -> p a n", a=2), psum[:, 4 * (t % 2):4 * (t % 2) + 2, :],
                                     ACT.Copy, scale=rms_y[:, t:t + 1]).then_inc(s_osb, 1)
                if t >= 1:
                    final_square(t - 1)
            final_square(TB - 1)

        @block.vector
        def _(dve):
            refined = [0]

            def inverse_root(y, v, s, t, number):
                steps = refined[0]
                dve.wait_ge(s_rs, number)
                nc.vector.reciprocal(y, s).then_inc(s_rn, 1)
                dve.wait_ge(s_rn, steps + 1)
                nc.vector.tensor_tensor(t, y, y, ALU.mult).then_inc(s_rn, 1)
                dve.wait_ge(s_rn, steps + 2)
                nc.vector.tensor_tensor(t, t, v, ALU.mult).then_inc(s_rn, 1)
                dve.wait_ge(s_rn, steps + 3)
                nc.vector.tensor_scalar(t, t, -0.5, 1.5, ALU.mult, ALU.add).then_inc(s_rn, 1)
                dve.wait_ge(s_rn, steps + 4)
                nc.vector.tensor_tensor(y, y, t, ALU.mult).then_inc(s_rn, 1)
                dve.wait_ge(s_rn, steps + 5)
                refined[0] += 5

            def mean_square(v, ss, n):
                nc.vector.tensor_scalar(v, ss, 1.0 / n, EPS, ALU.mult, ALU.add).then_inc(s_rv, 1)

            def normalise_x(h):
                dve.wait_ge(s_ssx, 4 * h + 4)
                mean_square(rms_v[:, 4 * h:4 * h + 4], ss_x[:, 4 * h:4 * h + 4], D)
                dve.wait_ge(s_rv, h + 1)
                inverse_root(rms_y[:, 4 * h:4 * h + 4], rms_v[:, 4 * h:4 * h + 4], rms_s[:, 4 * h:4 * h + 4],
                             rms_t[:, 4 * h:4 * h + 4], h + 1)
                for t in range(4):
                    nc.vector.tensor_scalar(work[:, t, :], work[:, t, :], rms_y[:, 4 * h + t:4 * h + t + 1], None,
                                            ALU.mult).then_inc(s_xn, 1)

            nc.vector.memset(ones[:], 1.0).then_inc(s_ones, 1)
            nc.vector.memset(ss_o, 0.0).then_inc(s_ones, 1)
            dve.wait_ge(s_const, 16 * 5)
            nc.vector.tensor_copy(ident_bf[:], ident[:]).then_inc(s_maskb, 1)
            dve.wait_ge(s_mask, 3)
            nc.vector.tensor_copy(mask_bf[:], mask_f[:]).then_inc(s_maskb, 1)
            normalise_x(0)
            dve.wait_ge(s_csig, 1)
            nc.vector.tensor_tensor(CUM[0], CUM[0], CUM[1], ALU.mult).then_inc(s_cact, 1)
            dve.wait_ge(s_cact, 1)

            def ada_column(n, c_act, junk, stage, slot, loads):
                dve.wait_ge(s_wa[slot], 16 * loads)
                if n >= 1:
                    dve.wait_ge(s_ada, n)
                nc.vector.tensor_tensor_reduce(out=junk, in0=stage, in1=c_act, scale=1.0, scalar=0.0,
                                               op0=ALU.mult, op1=ALU.add,
                                               accum_out=ada[:, n:n + 1]).then_inc(s_ada, 1)

            for n in range(2 * DC):
                ada_column(n, CUM[0], CUM[1], work[:, 6 + n % 3, :], n % 3, n // 3 + 1)
            dve.wait_ge(s_ada, 2 * DC)
            nc.vector.tensor_tensor(ada[:, 0:2 * DC], ada[:, 0:2 * DC], b_ada_sb[:, 0:2 * DC],
                                    ALU.add).then_inc(s_acol, 1)
            dve.wait_ge(s_acol, 1)
            nc.vector.tensor_scalar(a_cols[:], ada[:, DC:2 * DC], 1.0, None, ALU.add).then_inc(s_acol, 1)
            dve.wait_ge(s_acol, 2)
            nc.vector.tensor_tensor(a_cols[:], a_cols[:], g_norm_sb, ALU.mult).then_inc(s_acol, 1)
            dve.wait_ge(s_acol, 3)
            normalise_x(1)
            for n in range(2 * DC):
                dve.wait_ge(s_hhi, n + 1)
                if n >= 2:
                    dve.wait_ge(s_hlo, n - 1)
                d = n % DC
                nc.vector.tensor_scalar(CUM[1][:, (n % 2) * HALF:(n % 2 + 1) * HALF], psum[:, x_piece_bank(n), :],
                                        a_cols[:, d:d + 1], ada[:, d:d + 1], ALU.mult, ALU.add).then_inc(s_hf, 1)

            def proj_out(u):
                p, kind, th = units[u]
                bank = PROJ[u % 2]
                st = p % 2
                cols = slice(th * HALF, (th + 1) * HALF)
                if kind == "v":
                    return
                dve.wait_ge(s_phi, u + 1)
                if kind == "q":
                    for a in range(2):
                        last = nc.vector.scalar_tensor_tensor(
                            out=stacks[HD:P, st, a, 0, cols], in0=bank[a * HD:(a + 1) * HD, :], scalar=SCALE,
                            in1=stacks[0:HD, st, a, 0, cols].bitcast(fp32), op0=ALU.mult, op1=ALU.subtract)
                    last.then_inc(s_plo, 1)
                elif kind == "k":
                    for a in range(2):
                        for half in range(2):
                            last = nc.vector.tensor_tensor(
                                stacks[half * HD:(half + 1) * HD, st, a, 2, cols], bank[a * HD:(a + 1) * HD, :],
                                stacks[0:HD, st, a, 1, cols].bitcast(fp32), ALU.subtract)
                    last.then_inc(s_plo, 1)
                elif kind == "g":
                    nc.vector.scalar_tensor_tensor(out=G_T[:, cols], in0=bank, scalar=g_grp_sb[:, p_col(p):p_col(p) + 1],
                                                   in1=G_T[:, cols], op0=ALU.mult, op1=ALU.mult).then_inc(s_plo, 1)
                else:
                    if th == 0:
                        nc.vector.tensor_scalar(bf_neg, b_f_sb, -1.0, None, ALU.mult).then_inc(s_f, 1)
                        dve.wait_ge(s_f, 1)
                    nc.vector.tensor_scalar(G_T[0:8, cols], bank[0:8, :], -1.0, bf_neg, ALU.mult,
                                            ALU.add).then_inc(s_plo, 1)

            def p_col(p):
                return (p % 2) * (PAIRS // 2) + p // 2

            def scores_out(g):
                n = (g % TB + 1) * P
                if is_sb(g):
                    dve.wait_ge(s_sig, SB_PIECE[g, len(pieces(g)) - 1])
                    nc.vector.tensor_tensor_scan(R[g % 2][:, 0:n][:, ::-1], R[g % 2][:, 0:n][:, ::-1],
                                                 R[g % 2][:, 0:n][:, ::-1], 1.0, ALU.mult,
                                                 ALU.bypass).then_inc(s_scan, 1)
                    return
                k = FX_UNIT[g]
                slot = g % 2
                if g % TB == 0:
                    dve.wait_ge(s_cumb, 32 * (g // (2 * STEPS) + 1))
                dve.wait_ge(s_t, T_ITEM["T", g - 2, len(tgroups(g - 2)) - 1])
                if k > 2:
                    dve.wait_ge(s_max, k - 2)
                for j, (a, e) in enumerate(pieces(g)):
                    dve.wait_ge(s_score, S_PIECE[g, j])
                    nc.vector.tensor_tensor_reduce(
                        out=U[slot][:, a:e], in0=SCORE[(S_PIECE[g, j] - 1) % 3][:, 0:e - a],
                        in1=CUM[unit(g)[1]][:, a:e], scale=1.0, scalar=LOWEST, op0=ALU.add, op1=ALU.max,
                        accum_out=row_max[:, 2 * slot + j:2 * slot + j + 1]).then_inc(s_logit, 1)
                dve.wait_ge(s_logit, FX_PIECE[g, len(pieces(g)) - 1])
                nc.vector.tensor_reduce(neg_max[:, slot:slot + 1], row_max[:, 2 * slot:2 * slot + len(pieces(g))],
                                        op=ALU.max, axis=mybir.AxisListType.X, negate=True).then_inc(s_max, 1)

            def inverse_sum(g):
                dve.wait_ge(s_exp, FX_UNIT[g])
                nc.vector.reciprocal(row_inv[:, g % 2:g % 2 + 1], row_sum[:, g % 2:g % 2 + 1]).then_inc(s_inv, 1)

            def values_out(q):
                a = (q // (TB // 2)) % 2
                qb = (2 * q) % TB
                dve.wait_ge(s_pvs, q + 1)
                if q % (STEPS // 2) == 0 and q > 0:
                    dve.wait_ge(s_sq, q // (STEPS // 2))
                nc.vector.tensor_tensor(O_T[a * HD:(a + 1) * HD, qb * P:(qb + 2) * P], OUT[0:HD, 0:2 * P],
                                        o_shift[a * HD:(a + 1) * HD, q % 2, :], ALU.add).then_inc(s_pvd, 1)

            def vt_out(p):
                for j in range(2):
                    n = T_ITEM["V", p, j]
                    dve.wait_ge(s_thi, T_HI["V", p, j])
                    bank = TRANS[(n - 1) % 2].rearrange("p (b d) -> p b d", d=P)
                    for a in range(2):
                        last = nc.vector.tensor_tensor(v_stack[:, p % 2, a, 4 * j:4 * j + 4, HD:P],
                                                       bank[:, :, a * HD:(a + 1) * HD],
                                                       v_stack[:, p % 2, a, 4 * j:4 * j + 4, 0:HD].bitcast(fp32),
                                                       ALU.subtract)
                    last.then_inc(s_tfree, 1)

            def squares_out(p):
                n = T_ITEM["SS", p, 0]
                dve.wait_ge(s_t, n)
                if p >= 2:
                    dve.wait_ge(s_tfree, T_ITEM["SS", p - 2, 0])
                cols = slice((p % 2) * TB, (p % 2 + 1) * TB)
                nc.vector.tensor_tensor(ss_o[:, cols], TRANS[(n - 1) % 2][:, 0:TB], ss_o[:, cols],
                                        ALU.add).then_inc(s_tfree, 1)

            def pt_out(g):
                for j, (a, e) in enumerate(tgroups(g)):
                    n = T_ITEM["T", g, j]
                    dve.wait_ge(s_thi, T_HI["T", g, j])
                    bank = TRANS[(n - 1) % 2][:, 0:(e - a) * P].rearrange("p (b q) -> p b q", q=P)
                    q0 = (g % 2) * P
                    nc.vector.tensor_tensor(pt_lo[:, a:e, q0:q0 + P], bank, pt_hi[:, a:e, q0:q0 + P].bitcast(fp32),
                                            ALU.subtract).then_inc(s_tfree, 1)

            for u in range(2 * N_FIRST):
                proj_out(u)
            dve.wait_ge(s_plo, LO_UNITS[-1, "f", 1])
            nc.vector.tensor_scalar(G_T[0:8, :], G_T[0:8, :], 0.0, None, ALU.max).then_inc(s_f, 1)
            dve.wait_ge(s_f, 2)
            dve.wait_ge(s_fa, 2)
            nc.vector.tensor_tensor_scan(CUM[0][0:8, :], G_T[0:8, :], CUM[1][0:8, :], 0.0, ALU.add,
                                         ALU.add).then_inc(s_f, 2)
            scores_out(0)
            scores_out(1)
            for g in range(UNITS):
                p, i = g // STEPS, g % STEPS
                if g + 1 < UNITS and not is_sb(g + 1):
                    inverse_sum(g + 1)
                u = 2 * N_FIRST + 8 * p + i // 2
                if i % 2 == 1 and u < len(units):
                    proj_out(u)
                if g % 2 == 0 and g >= 2:
                    values_out(g // 2 - 1)
                if i == 0:
                    vt_out(p)
                if i == 4 and p >= 1:
                    squares_out(p - 1)
                pt_out(g)
                if g + 2 < UNITS:
                    scores_out(g + 2)
            values_out(GROUPS - 1)

            dve.wait_ge(s_csig, 2)
            nc.vector.tensor_tensor(CUM[1], CUM[1], CUM[0], ALU.mult).then_inc(s_cact, 1)
            dve.wait_ge(s_cact, 2)
            loads = [len(range(s, 2 * DC, 3)) for s in range(2)]
            for n in range(DC):
                hi, lo = y_parts(n)
                dve.wait_ge(s_yld[n % 2], 16 * (n // 2 + 1))
                nc.vector.tensor_copy(hi, R[n % 2]).then_inc(s_yhi, 1)
                ada_column(2 * DC + n, CUM[1], CUM[0], U[n % 2], n % 2, loads[n % 2] + n // 2 + 1)
                dve.wait_ge(s_yhi, n + 1)
                nc.vector.tensor_tensor(lo, R[n % 2], hi.bitcast(fp32), ALU.subtract).then_inc(s_ylo, 1)
            dve.wait_ge(s_ada, 3 * DC)
            nc.vector.scalar_tensor_tensor(out=a_cols[:], in0=ada[:, 2 * DC:3 * DC], scalar=1.0,
                                           in1=b_ada_sb[:, 2 * DC:3 * DC], op0=ALU.add,
                                           op1=ALU.add).then_inc(s_gate, 1)
            squares_out(PAIRS - 1)
            dve.wait_ge(s_tfree, T_ITEM["SS", PAIRS - 1, 0])
            mean_square(rms_v[:], ss_o, N_TYPE)
            dve.wait_ge(s_rv, 3)
            inverse_root(rms_y[:], rms_v[:], rms_s[:], rms_t[:], 3)
            dve.wait_ge(s_row, 32)
            for t in range(TB):
                slot = t % 2
                dve.wait_ge(s_osb, t + 1)
                if t >= 2:
                    dve.wait_ge(s_store[slot], 16 * (t // 2))
                nc.vector.scalar_tensor_tensor(out=R[slot].rearrange("p (a n) -> p a n", a=2),
                                               in0=psum[:, 4 * slot + 2:4 * slot + 4, :],
                                               scalar=rms_y[:, TB + t:TB + t + 1],
                                               in1=U[slot].rearrange("p (a n) -> p a n", a=2), op0=ALU.mult,
                                               op1=ALU.add).then_inc(s_ofx, 1)
                dve.wait_ge(s_ofx, t + 1)
                nc.vector.tensor_tensor(R[slot], R[slot], CUM[0], ALU.mult).then_inc(s_fin, 1)
                dve.wait_ge(s_fin, 2 * t + 1)
                dve.wait_ge(s_xr[slot], 16 * (t // 2 + 1))
                nc.vector.tensor_tensor(R[slot], R[slot], work[:, 6 + slot, :], ALU.add).then_inc(s_fin, 1)
                dve.wait_ge(s_fsq, t + 1)
                mean_square(row_max[:, slot:slot + 1], ss_x[:, t:t + 1], D)
                dve.wait_ge(s_rv, 4 + t)
                inverse_root(row_inv[:, slot:slot + 1], row_max[:, slot:slot + 1], row_sum[:, slot:slot + 1],
                             neg_max[:, slot:slot + 1], 4 + t)
                nc.vector.scalar_tensor_tensor(out=R[slot], in0=R[slot], scalar=row_inv[:, slot:slot + 1],
                                               in1=CUM[1], op0=ALU.mult, op1=ALU.mult).then_inc(s_done, 1)

        @block.tensor
        def _(pe):
            pe.wait_ge(s_const, 16 * 5)
            pe.wait_ge(s_xn, 4)

            def transpose_x(n):
                th, d = n // DC, n % DC
                if n >= 8:
                    pe.wait_ge(s_xn, 8)
                    pe.wait_ge(s_hf, n - 5)
                for t in range(4):
                    last = nc.tensor.transpose(psum[:, x_piece_bank(n), t * P:(t + 1) * P],
                                               work[:, t, d * P:(d + 1) * P], ident[:])
                last.then_inc(s_xt, 1)

            for n in range(2 * DC):
                transpose_x(n)

            def proj(u, first, last_chunk):
                p, kind, th = units[u]
                b = u // 2
                bank = PROJ[u % 2]
                cols = slice(th * HALF, (th + 1) * HALF)
                if first == 0:
                    pe.wait_ge(s_wlo, b + 1)
                    if u == 0:
                        pe.wait_ge(s_hlo, 2 * DC)
                    if u >= 2:
                        before = units[u - 2]
                        if before[1] == "v":
                            pe.wait_ge(s_phi, u - 1)
                        else:
                            pe.wait_ge(s_plo, LO_UNITS[before])
                for c_ in range(first, last_chunk):
                    hi = w_hi[:, w_slot(b), c_, :]
                    lo = w_lo[:, w_slot(b), c_, :]
                    nc.tensor.matmul(bank, hi, h_hi[:, c_, cols], start=(c_ == 0), stop=False)
                    nc.tensor.matmul(bank, hi, h_lo[:, c_, cols], start=False, stop=False)
                    last = nc.tensor.matmul(bank, lo, h_hi[:, c_, cols], start=False, stop=(c_ == DC - 1))
                if last_chunk == DC:
                    last.then_inc(s_proj, 1)

            def scores(g):
                p, a, qb = unit(g)
                q = stacks[:, p % 2, a, 0, qb * P:(qb + 1) * P]
                if g % STEPS == 0:
                    pe.wait_ge(s_plo, LO_UNITS[p, "k", 1])
                for j, (c0, c1) in enumerate(pieces(g)):
                    n = S_PIECE[g, j]
                    bank = SCORE[(n - 1) % 3]
                    if n > 3:
                        before = piece_list[n - 4]
                        if is_sb(before[0]):
                            pe.wait_ge(s_sig, SB_PIECE[before])
                        else:
                            pe.wait_ge(s_logit, FX_PIECE[before])
                    diagonal = c1 == (qb + 1) * P
                    nc.tensor.matmul(bank[:, 0:c1 - c0], q, stacks[:, p % 2, a, 1, c0:c1], start=True, stop=False)
                    last = nc.tensor.matmul(bank[:, 0:c1 - c0], q, stacks[:, p % 2, a, 2, c0:c1], start=False,
                                            stop=not diagonal)
                    if diagonal:
                        last = nc.tensor.matmul(bank[:, c1 - c0 - P:c1 - c0], ident_bf[:],
                                                mask_bf[:, 0 if is_sb(g) else 1, :], start=False, stop=True)
                    last.then_inc(s_score, 1)

            def next_bank(item):
                n = T_ITEM[item]
                if n > 2:
                    pe.wait_ge(s_tfree, n - 2)
                return TRANS[(n - 1) % 2]

            def transpose_v(p):
                pe.wait_ge(s_phi, unit_no[p, "v", 1] + 1)
                for j in range(2):
                    bank = next_bank(("V", p, j))
                    for k in range(4):
                        last = nc.tensor.transpose(bank[:, k * P:(k + 1) * P],
                                                   VT[:, (4 * j + k) * P:(4 * j + k + 1) * P], ident[:])
                    last.then_inc(s_t, 1)

            def transpose_probs(g):
                pe.wait_ge(s_prob, g + 1)
                for j, (a, e) in enumerate(tgroups(g)):
                    bank = next_bank(("T", g, j))
                    for k in range(a, e):
                        last = nc.tensor.transpose(bank[:, (k - a) * P:(k - a + 1) * P],
                                                   U[g % 2][:, k * P:(k + 1) * P], ident[:])
                    last.then_inc(s_t, 1)

            def sum_squares(p):
                pe.wait_ge(s_sq, p + 1)
                bank = next_bank(("SS", p, 0))
                for t in range(TB):
                    last = nc.tensor.matmul(bank[:, t:t + 1], VT[:, t * P:(t + 1) * P], ones[:], start=True, stop=True)
                last.then_inc(s_t, 1)

            def values(q):
                p, a, qb = unit(2 * q)
                g = 2 * q + 1
                pe.wait_ge(s_tfree, T_ITEM["T", g, len(tgroups(g)) - 1])
                if q >= 1:
                    pe.wait_ge(s_pvd, q)
                for k in range(qb + 2):
                    c0 = 0 if k <= qb else P
                    for n, src in enumerate((pt_hi, pt_lo)):
                        last = nc.tensor.matmul(OUT[:, c0:2 * P], v_stack[:, p % 2, a, k, :], src[:, k, c0:2 * P],
                                                start=(k == 0 and n == 0), stop=(k == qb + 1 and n == 1))
                last.then_inc(s_pv, 1)

            for u in range(2 * N_FIRST):
                proj(u, 0, DC)
            pe.wait_ge(s_maskb, 2)
            scores(0)
            scores(1)
            for g in range(UNITS):
                p, i = g // STEPS, g % STEPS
                u = 2 * N_FIRST + 8 * p + i // 2
                if u < len(units) and (p + 1 < PAIRS or i < 4):
                    proj(u, (i % 2) * DC // 2, (i % 2 + 1) * DC // 2)
                if g % 2 == 0 and g >= 2:
                    values(g // 2 - 1)
                if i == 0:
                    transpose_v(p)
                if i == 4 and p >= 1:
                    sum_squares(p - 1)
                if g + 2 < UNITS:
                    scores(g + 2)
                transpose_probs(g)
            values(GROUPS - 1)
            sum_squares(PAIRS - 1)

            pe.wait_ge(s_wlo, len(blocks) + DC)
            pe.wait_ge(s_tfree, T_ITEM["SS", PAIRS - 1, 0])
            for t in range(TB):
                if t >= 2:
                    pe.wait_ge(s_ofx, t - 1)
                for kind in range(2):
                    for j in range(PAIRS // 2):
                        p = 2 * j + kind
                        if t == 0:
                            pe.wait_ge(s_ylo, PAIRS if kind == 1 else p + 1)
                        m = kind * (PAIRS // 2) + j
                        hi, lo = y_parts(p)
                        yh, yl = hi[:, t * P:(t + 1) * P], lo[:, t * P:(t + 1) * P]
                        for y_, w_, k in ((yh, h_hi, 0), (yh, h_lo, 1), (yl, h_hi, 2)):
                            for half in range(2):
                                last = nc.tensor.matmul(psum[:, 4 * (t % 2) + 2 * kind + half, :], y_,
                                                        w_[:, m, half * HALF:(half + 1) * HALF],
                                                        start=(j == 0 and k == 0),
                                                        stop=(j == PAIRS // 2 - 1 and k == 2))
                last.then_inc(s_op, 1)


def kernel(x, c, w_ada, b_ada, g_norm, w_in, b_f, g_grp, w_out, g_final):
    import concourse.bacc as bacc
    from concourse.bass_utils import run_bass_kernel_spmd

    def columns(v):
        return np.ascontiguousarray(np.asarray(v).reshape(-1, 128).T)

    x = np.asarray(x)
    batch, seq, d = x.shape
    arrays = {
        "in_x": np.ascontiguousarray(x[0]),
        "in_c": np.ascontiguousarray(c),
        "in_w_ada_t": np.ascontiguousarray(np.asarray(w_ada)[0].T),
        "in_b_ada": columns(b_ada),
        "in_g_norm": columns(g_norm),
        "in_w_in": np.ascontiguousarray(np.asarray(w_in)[0]),
        "in_b_f": np.ascontiguousarray(np.asarray(b_f).reshape(-1, 1)),
        "in_g_grp": columns(g_grp),
        "in_w_out": np.ascontiguousarray(np.asarray(w_out)[0]),
        "in_g_final": np.ascontiguousarray(np.asarray(g_final).reshape(1, -1)),
        "in_identity": np.eye(128, dtype=np.float32),
    }
    nc = bacc.Bacc("TRN2", target_bir_lowering=False, num_devices=1)
    args = [nc.dram_tensor(n, a.shape, mybir.dt.from_np(a.dtype), kind="ExternalInput").ap()
            for n, a in arrays.items()]
    out = nc.dram_tensor("out_x", (seq, d), mybir.dt.float32, kind="ExternalOutput").ap()
    hybrid_trunk_kernel(nc, *args, out)
    got = run_bass_kernel_spmd(nc, [arrays], core_ids=[0])
    return got.results[0]["out_x"].reshape(batch, seq, d)
```

```python
from contextlib import ExitStack

import numpy as np

import concourse.bass as bass
from concourse import mybir


def hybrid_trunk_kernel(nc, x, c, w_ada_t, b_ada_cols, g_norm_cols, w_in, b_f_col, g_grp_cols, w_out, g_final,
                        identity, out):
    fp32 = mybir.dt.float32
    fp32r = mybir.dt.float32r
    bf16 = mybir.dt.bfloat16
    ALU = mybir.AluOpType
    ACT = mybir.ActivationFunctionType

    P = 128
    SEQ, D = x.shape
    HD = 64
    DC = D // P
    TB = SEQ // P
    HALF = 512
    NHALF = SEQ // HALF
    N_TYPE = 512
    PAIRS = 2 * N_TYPE // P
    STEPS = 2 * TB
    UNITS = PAIRS * STEPS
    GROUPS = UNITS // 2
    EPS = 1e-6
    MASKED = -1e30
    SCALE = HD ** -0.5
    LOWEST = -3e38

    def is_sb(g):
        return (g // STEPS) % 2 == 0

    def unit(g):
        return g // STEPS, (g % STEPS) // TB, g % TB

    def pieces(g):
        n = (g % TB + 1) * P
        return [(a, min(a + HALF, n)) for a in range(0, n, HALF)]

    def tgroups(g):
        n = g % TB + 1
        return [(a, min(a + 4, n)) for a in range(0, n, 4)]

    def numbered(events):
        return {e: i + 1 for i, e in enumerate(events)}

    blocks = [(0, "q"), (0, "k"), (0, "v"), (-1, "f")]
    for p in range(PAIRS):
        if p + 1 < PAIRS:
            blocks += [(p + 1, "q"), (p + 1, "k"), (p, "g"), (p + 1, "v")]
        else:
            blocks += [(p, "g")]
    N_FIRST = 4
    units = [(0, "q", 0), (0, "k", 0), (0, "q", 1), (0, "k", 1)]
    units += [(p, kind, h) for p, kind in blocks[2:] for h in range(NHALF)]
    block_no = {b: i for i, b in enumerate(blocks)}
    unit_no = {u: i for i, u in enumerate(units)}
    k_units = [i for i, u in enumerate(units) if u[1] == "k"]

    def w_columns(p, kind):
        t, j = p % 2, p // 2
        if kind == "f":
            return w_in[:, 8 * N_TYPE:8 * N_TYPE + 8], 8
        base = 6 * N_TYPE + t * N_TYPE if kind == "g" else (3 * t + "qkv".index(kind)) * N_TYPE
        return w_in[:, base + P * j:base + P * (j + 1)], P

    all_units = list(range(UNITS))
    S_PIECE = numbered([(g, j) for g in all_units for j in range(len(pieces(g)))])
    SB_PIECE = numbered([(g, j) for g in all_units if is_sb(g) for j in range(len(pieces(g)))])
    FX_PIECE = numbered([(g, j) for g in all_units if not is_sb(g) for j in range(len(pieces(g)))])
    SB_UNIT = numbered([g for g in all_units if is_sb(g)])
    FX_UNIT = numbered([g for g in all_units if not is_sb(g)])
    piece_list = list(S_PIECE)

    def squares_step(p):
        return 3 if p == PAIRS - 1 else 4

    V_STEPS = [STEPS - 1, 1]
    t_items = [("V", 0, 0)]
    for g in all_units + [UNITS]:
        p, i = g // STEPS, g % STEPS
        if g < UNITS and i == V_STEPS[0] and p + 1 < PAIRS:
            t_items.append(("V", p + 1, 0))
        if g < UNITS and i == V_STEPS[1]:
            t_items.append(("V", p, 1))
        if g == UNITS or p >= 1 and i == squares_step(p):
            t_items.append(("SS", p - 1, 0))
        if g < UNITS:
            t_items += [("T", g, j) for j in range(len(tgroups(g)))]
    T_ITEM = numbered(t_items)
    T_HI = numbered([e for e in t_items if e[0] != "SS"])
    LO_UNITS = numbered([u for u in units if u[1] != "v"])
    LAST = PAIRS - 1
    Y_SPLIT = numbered([LAST - 1, LAST])

    jobs = [("w", h, m) for h in range(NHALF) for m in range(DC)]
    jobs += [("y", h, m) for m in range(LAST - 2) for h in range(NHALF)]
    job_steps = [(p, i) for p in (1, 3) for i in (1, 2, 5, 6, 8, 9, 10, 12)]
    job_steps += [(LAST - 2, i) for i in (1, 2, 3, 5, 6, 7, 9, 10, 11, 12)]
    JOB_AT = dict(zip(job_steps, range(len(jobs))))
    JOBS_BY = {p: sum(q <= p for q, _ in job_steps) for p in range(-1, PAIRS)}

    QUARTERS = 4
    QUARTER_AT = {(LAST - 1, 3 + 3 * k): k for k in range(QUARTERS)}

    STORED = 3
    sb_tiles = [(t + TB - STORED) % TB for t in range(TB)]
    sb_units = [(sb_tiles[t], h) for t, h in ((0, 0), (1, 0), (0, 1), (1, 1))]
    sb_units += [(t, h) for t in sb_tiles[2:] for h in range(2)]
    SB_FROM = 5
    SB_AT = {i: range((i - SB_FROM) * len(sb_units) // (STEPS - SB_FROM),
                      (i - SB_FROM + 1) * len(sb_units) // (STEPS - SB_FROM)) for i in range(SB_FROM, STEPS)}
    SB_NO = numbered(sb_units)
    X_AT = {1: (0, 1, 2), 3: (3,), 6: (4,)}

    x_tiles = x.rearrange("(t p) d -> t p d", p=P)
    out_tiles = out.rearrange("(t p) d -> t p d", p=P)
    ada_tiles = w_ada_t.rearrange("(n p) k -> n p k", p=P)
    wo_tiles = w_out.rearrange("(m p) n -> m p n", p=P)

    ctx = ExitStack()
    with ctx:
        def sb(name, shape, dt=fp32):
            return ctx.enter_context(nc.sbuf_tensor(name, shape, dt))

        def sem(name):
            return ctx.enter_context(nc.semaphore(name))

        y_dram = nc.dram_tensor("y_scratch", (PAIRS, P, SEQ), fp32, kind="Internal").ap()
        y_split_dram = nc.dram_tensor("y_split_scratch", (PAIRS, P, 2, SEQ), fp32, kind="Internal").ap()
        w_split_dram = nc.dram_tensor("w_split_scratch", (NHALF, 2, P, DC, HALF), fp32, kind="Internal").ap()
        c_dram = nc.dram_tensor("forget_scratch", (8, SEQ), fp32, kind="Internal").ap()
        sb_dram = nc.dram_tensor("sb_out_scratch", (TB, P, D), fp32, kind="Internal").ap()
        gate_dram = nc.dram_tensor("gate_scratch", (1, D), fp32, kind="Internal").ap()

        h_hi = sb("h_hi", [P, DC, SEQ], fp32r)
        h_lo = sb("h_lo", [P, DC, SEQ], fp32r)
        w_raw = sb("w_raw", [P, DC, P])
        w_hi = sb("w_hi", [P, 2, DC, P], fp32r)
        w_lo = sb("w_lo", [P, 2, DC, P], fp32r)
        stacks = sb("stacks", [P, 2, 2, 3, SEQ], fp32r)
        v_stack = sb("v_stack", [P, 2, 2, TB, P], fp32r)
        pt_hi = sb("pt_hi", [P, TB, 2 * P], fp32r)
        pt_lo = sb("pt_lo", [P, TB, 2 * P], fp32r)
        work = sb("work", [P, 9, SEQ])
        U = [work[:, 0, :], work[:, 1, :]]
        R = [work[:, 2, :], work[:, 3, :]]
        CUM = [work[:, 4, :], work[:, 5, :]]
        VT = work[:, 6, :]
        O_T = work[:, 7, :]
        G_T = work[:, 8, :]
        gate_half = sb("gate_half", [P, HALF])
        o_shift = sb("o_shift", [P, 2, 2 * P])
        ident = sb("ident", [P, P])
        ident_bf = sb("ident_bf", [P, P], bf16)
        mask_f = sb("mask_f", [P, 2, P])
        mask_bf = sb("mask_bf", [P, 2, P], bf16)
        ones = sb("ones", [P, 1])
        small = sb("small", [P, 192])
        ada = small[:, 0:24]
        b_ada_sb = small[:, 24:48]
        g_norm_sb = small[:, 48:56]
        g_grp_sb = small[:, 56:64]
        a_cols = small[:, 64:72]
        ss_x = small[:, 72:80]
        rms_v = small[:, 80:96]
        rms_s = small[:, 96:112]
        rms_y = small[:, 112:128]
        rms_t = small[:, 128:144]
        ss_o = small[:, 144:160]
        b_f_sb = small[0:8, 160:161]
        row_max = small[:, 164:168]
        neg_max = small[:, 168:170]
        row_sum = small[:, 170:172]
        row_inv = small[:, 172:174]
        bf_neg = small[0:8, 174:175]

        psum = ctx.enter_context(nc.psum_tensor("psum", [P, 8, 512], fp32))
        PROJ = [psum[:, 0, :], psum[:, 1, :]]
        SCORE = [psum[:, 2, :], psum[:, 3, :], psum[:, 4, :]]
        TRANS = [psum[:, 5, :], psum[:, 6, :]]
        OUT = psum[:, 7, :]

        s_const = sem("s_const")
        s_x = [sem(f"s_x{i}") for i in range(4)]
        s_wa = [sem(f"s_wa{i}") for i in range(4)]
        s_c = sem("s_c")
        s_csig = sem("s_csig")
        s_cact = sem("s_cact")
        s_ada = sem("s_ada")
        s_acol = sem("s_acol")
        s_ssx = sem("s_ssx")
        s_rv = sem("s_rv")
        s_rs = sem("s_rs")
        s_rn = sem("s_rn")
        s_xn = sem("s_xn")
        s_xt = sem("s_xt")
        s_hhi = sem("s_hhi")
        s_hf = sem("s_hf")
        s_hlo = sem("s_hlo")
        s_mask = sem("s_mask")
        s_maskb = sem("s_maskb")
        s_ones = sem("s_ones")
        s_wraw = sem("s_wraw")
        s_whi = sem("s_whi")
        s_wlo = sem("s_wlo")
        s_proj = sem("s_proj")
        s_phk = sem("s_phk")
        s_phi = sem("s_phi")
        s_plo = sem("s_plo")
        s_f = sem("s_f")
        s_fa = sem("s_fa")
        s_cum = sem("s_cum")
        s_cumb = sem("s_cumb")
        s_score = sem("s_score")
        s_sig = sem("s_sig")
        s_scan = sem("s_scan")
        s_logit = sem("s_logit")
        s_max = sem("s_max")
        s_exp = sem("s_exp")
        s_inv = sem("s_inv")
        s_prob = sem("s_prob")
        s_t = sem("s_t")
        s_thi = sem("s_thi")
        s_tfree = sem("s_tfree")
        s_pv = sem("s_pv")
        s_pvs = sem("s_pvs")
        s_pvd = sem("s_pvd")
        s_y = sem("s_y")
        s_sq = sem("s_sq")
        s_yst = sem("s_yst")
        s_yhi = sem("s_yhi")
        s_ylo = sem("s_ylo")
        s_grow = sem("s_grow")
        s_jld = [sem(f"s_jld{i}") for i in range(2)]
        s_jsc = sem("s_jsc")
        s_jhi = sem("s_jhi")
        s_jlo = sem("s_jlo")
        s_qld = sem("s_qld")
        s_qhi = sem("s_qhi")
        s_qlo = sem("s_qlo")
        s_qst = sem("s_qst")
        s_jst = [sem(f"s_jst{i}") for i in range(2)]
        s_ypl = [sem(f"s_ypl{i}") for i in range(PAIRS - 2)]
        s_wol = [sem(f"s_wol{i}") for i in range(4)]
        s_zst = [sem(f"s_zst{i}") for i in range(STORED)]
        s_zld = [sem(f"s_zld{i}") for i in range(STORED)]
        s_wg = [sem(f"s_wg{i}") for i in range(4)]
        s_id = sem("s_id")
        s_gate = sem("s_gate")
        s_gst = sem("s_gst")
        s_row = sem("s_row")
        s_op = sem("s_op")
        s_opb = sem("s_opb")
        s_osb = sem("s_osb")
        s_fin = sem("s_fin")
        s_fsq = sem("s_fsq")
        s_done = sem("s_done")
        s_xr = [sem(f"s_xr{i}") for i in range(TB)]
        s_store = [sem(f"s_store{i}") for i in range(TB)]

        block = ctx.enter_context(nc.Block())

        XBANK = [0, 1, 2, 3, 4, 5, 6, 7]

        def x_piece_bank(n):
            return XBANK[n] if n < 8 else XBANK[2 + (n - 8) % 6]

        def w_slot(b):
            return b % 2

        def y_parts(m):
            kind, j = m % 2, m // 2
            if kind == 0 and j < 3:
                flat = stacks[:, 0, :, :, :].rearrange("p h s n -> p (h s) n")
                return flat[:, 2 * j + 1, :], flat[:, 2 * j, :]
            if kind == 0:
                flat = v_stack[:, 0, :, :, :].rearrange("p h b n -> p h (b n)")
                return flat[:, 0, :], flat[:, 1, :]
            if j < 2:
                return tuple(w[:, j].rearrange("p c n -> p (c n)") for w in (w_hi, w_lo))
            return stacks[:, 1, j - 2, 1, :], stacks[:, 1, j - 2, 0, :]

        w_flat = w_raw[:].rearrange("p c n -> p (c n)")
        GATE_LAST = w_flat
        Z = [G_T, R[0], R[1], VT, CUM[0], G_T, R[0], R[1]]
        RES = Z[STORED:] + [U[1], O_T, U[0]]
        SQUARES = U[0]

        def gate_of(p):
            return GATE_LAST if p == LAST else G_T
        WA_SLOT = [6, 7, 8, 5]

        @block.sync
        def _(sp):
            sp.dma_start(CUM[0], c[0:1, :].partition_broadcast(P)).then_inc(s_c, 16)
            for t in range(4):
                sp.dma_start(work[:, t, :], x_tiles[t]).then_inc(s_x[t], 16)
            def load_w(b):
                p, kind = blocks[b]
                src, n = w_columns(p, kind)
                if b >= 1:
                    sp.wait_ge(s_wlo, b)
                sp.dma_start(w_raw[:, :, 0:n], src.rearrange("(c p) n -> p c n", p=P)).then_inc(s_wraw, 16)

            for n in range(2 * DC):
                if n == 3:
                    sp.wait_ge(s_cact, 1)
                if n >= 4:
                    sp.wait_ge(s_ada, n - 3)
                sp.dma_start(work[:, WA_SLOT[n % 4], :], ada_tiles[n]).then_inc(s_wa[n % 4], 16)
                if n == 3 or n == 7:
                    load_w(n // 4)
            sp.wait_ge(s_xt, DC)
            for t in range(4):
                sp.dma_start(work[:, t, :], x_tiles[4 + t]).then_inc(s_x[t], 16)
            load_w(2)

            def load_gate(n):
                sp.dma_start(work[:, n % 4, :], ada_tiles[2 * DC + n]).then_inc(s_wg[n % 4], 16)

            sp.wait_ge(s_xt, 2 * DC)
            for n in range(4):
                load_gate(n)
            load_w(3)
            for n in range(4, DC):
                sp.wait_ge(s_ada, 2 * DC + n - 3)
                load_gate(n)
            load_w(N_FIRST)
            sp.wait_ge(s_gate, 1)
            sp.dma_start(gate_dram.rearrange("a (b p) -> p (a b)", p=P), a_cols,
                         allow_slow_non_contiguous=True).then_inc(s_gst, 16)
            sp.wait_ge(s_f, 4)
            sp.dma_start(c_dram, CUM[0][0:8, :]).then_inc(s_cum, 16)

            def load_job(n):
                kind, half, m = jobs[n]
                cols = slice(half * HALF, (half + 1) * HALF)
                slot = n % 2
                if (n - 1) // DC != n // DC and kind == "w":
                    sp.wait_ge(s_gst, 16)
                    if n > 0:
                        sp.wait_ge(s_jlo, n)
                    sp.dma_start(gate_half[:], gate_dram[0:1, cols].partition_broadcast(P)).then_inc(s_grow, 16)
                p = job_steps[n][0]
                if n == JOBS_BY[p - 1]:
                    sp.wait_ge(s_prob, p * STEPS)
                if n >= 2:
                    sp.wait_ge(s_jst[slot], 16 * (n // 2))
                if kind == "y":
                    sp.wait_ge(s_yst, 16 * (m + 1))
                src = wo_tiles[m] if kind == "w" else y_dram[m]
                sp.dma_start(R[slot][:, 0:HALF], src[:, cols]).then_inc(s_jld[slot], 16)

            def store_job(n):
                kind, half, m = jobs[n]
                slot = n % 2
                sp.wait_ge(s_jlo, n + 1)
                dst = (w_split_dram[half, :, :, m, :].rearrange("s p n -> p s n") if kind == "w"
                       else y_split_dram[m, :, :, half * HALF:(half + 1) * HALF])
                sp.dma_start(dst, R[slot].rearrange("p (s n) -> p s n", s=2)).then_inc(s_jst[slot], 16)

            def quarter(k):
                width = SEQ // QUARTERS
                if k >= 1:
                    sp.wait_ge(s_qlo, k)
                    sp.dma_start(y_split_dram[LAST - 2, :, :, (k - 1) * width:k * width],
                                 gate_half[:].rearrange("p (s n) -> p s n", s=2)).then_inc(s_qst, 16)
                if k < QUARTERS:
                    if k == 0:
                        sp.wait_ge(s_jlo, 2 * DC)
                        sp.wait_ge(s_yst, 16 * (LAST - 1))
                    else:
                        sp.wait_ge(s_qst, 16 * k)
                    sp.dma_start(gate_half[:, 0:width],
                                 y_dram[LAST - 2, :, k * width:(k + 1) * width]).then_inc(s_qld, 16)

            def load_x_again(n):
                if n == 0:
                    sp.wait_ge(s_ylo, Y_SPLIT[LAST - 1])
                    for slot in range(2):
                        sp.wait_ge(s_jst[slot], 16 * len(range(slot, len(jobs), 2)))
                    sp.wait_ge(s_prob, LAST * STEPS)
                if n == 3:
                    sp.wait_ge(s_tfree, T_ITEM["SS", LAST - 1, 0])
                if n == 4:
                    sp.wait_ge(s_logit, FX_PIECE[LAST * STEPS + TB - 1, 1])
                if n >= 5:
                    sp.wait_ge(s_zst[n - 5], 16)
                sp.dma_start(Z[n], x_tiles[sb_tiles[n]]).then_inc(s_xr[n], 16)

            def store_z(n):
                sp.wait_ge(s_osb, SB_NO[sb_tiles[n], 1])
                sp.dma_start(sb_dram[n], Z[n]).then_inc(s_zst[n], 16)

            pending = []
            for g in range(UNITS):
                p, i = g // STEPS, g % STEPS
                b = N_FIRST + 4 * p + i // 4 + 1
                if i % 4 == 0 and b < len(blocks):
                    load_w(b)
                if (p, i) in JOB_AT:
                    if len(pending) == 2:
                        store_job(pending.pop(0))
                    load_job(JOB_AT[p, i])
                    pending.append(JOB_AT[p, i])
                elif pending:
                    store_job(pending.pop(0))
                if (p, i) in QUARTER_AT:
                    quarter(QUARTER_AT[p, i])
                if p == LAST:
                    if i == 0:
                        quarter(QUARTERS)
                    if i in X_AT:
                        for n in X_AT[i]:
                            load_x_again(n)
                    for n in SB_AT.get(i - 1, ()):
                        t, h = sb_units[n]
                        k = sb_tiles.index(t)
                        if h == 1 and k < STORED:
                            store_z(k)
                            load_x_again(k + 5)
                if i == 2 and 1 <= p < LAST:
                    sp.wait_ge(s_y, p)
                    sp.dma_start(y_dram[p - 1], G_T).then_inc(s_yst, 16)
                if i == 3 and p % 2 == 0:
                    sp.wait_ge(s_cum, 16)
                    if p >= 2:
                        sp.wait_ge(s_logit, FX_PIECE[p * STEPS - 1, 1])
                    for a in range(2):
                        sp.dma_start(CUM[a], c_dram[p + a:p + a + 1, :].partition_broadcast(P)).then_inc(s_cumb, 16)

            def load_z(n):
                sp.wait_ge(s_zst[n], 16)
                sp.dma_start(RES[sb_tiles[n]], sb_dram[n]).then_inc(s_zld[n], 16)

            sp.wait_ge(s_logit, FX_PIECE[UNITS - 1, 1])
            sp.dma_start(CUM[1], g_final[0:1, :].partition_broadcast(P)).then_inc(s_row, 16)
            sp.wait_ge(s_t, T_ITEM["T", UNITS - 1, 1])
            load_z(0)
            sp.wait_ge(s_sq, PAIRS)
            sp.wait_ge(s_y, PAIRS)
            load_z(1)
            sp.wait_ge(s_t, T_ITEM["SS", LAST, 0])
            load_z(2)
            for t in range(TB):
                sp.wait_ge(s_store[t], 16)

        @block.gpsimd
        def _(pool):
            nc.gpsimd.memset(mask_f[:], 0.0).then_inc(s_mask, 1)
            pool.wait_ge(s_mask, 1)
            nc.gpsimd.affine_select(out=mask_f[:, 0, :], in_=mask_f[:, 0, :], compare_op=ALU.is_gt, fill=MASKED,
                                    base=0, pattern=[[-1, P]], channel_multiplier=1).then_inc(s_mask, 1)
            nc.gpsimd.affine_select(out=mask_f[:, 1, :], in_=mask_f[:, 1, :], compare_op=ALU.is_ge, fill=MASKED,
                                    base=0, pattern=[[-1, P]], channel_multiplier=1).then_inc(s_mask, 1)

            def split_w(b):
                if b >= 2:
                    pool.wait_ge(s_proj, unit_no[blocks[b - 2] + (1,)] + 1)
                pool.wait_ge(s_wraw, 16 * (b + 1))
                nc.gpsimd.tensor_scalar(w_hi[:, w_slot(b)], w_raw[:], 1.0, 1.0, ALU.mult, ALU.mult).then_inc(s_whi, 1)
                pool.wait_ge(s_whi, b + 1)
                nc.gpsimd.tensor_tensor(w_lo[:, w_slot(b)], w_raw[:], w_hi[:, w_slot(b)].bitcast(fp32),
                                        ALU.subtract).then_inc(s_wlo, 1)

            def do_job(n):
                kind, half, m = jobs[n]
                slot = n % 2
                piece, hi = R[slot][:, 0:HALF], R[slot][:, HALF:2 * HALF]
                pool.wait_ge(s_jld[slot], 16 * (n // 2 + 1))
                if kind == "w":
                    pool.wait_ge(s_grow, 16 * (half + 1))
                    nc.gpsimd.tensor_tensor(piece, piece, gate_half[:], ALU.mult).then_inc(s_jsc, 1)
                    pool.wait_ge(s_jsc, n + 1)
                nc.gpsimd.tensor_scalar(hi.bitcast(fp32r), piece, 1.0, 1.0, ALU.mult, ALU.mult).then_inc(s_jhi, 1)
                pool.wait_ge(s_jhi, n + 1)
                nc.gpsimd.tensor_tensor(piece.bitcast(fp32r), piece, hi, ALU.subtract).then_inc(s_jlo, 1)

            def split_quarter(k):
                width = SEQ // QUARTERS
                piece, hi = gate_half[:, 0:width], gate_half[:, width:2 * width]
                pool.wait_ge(s_qld, 16 * (k + 1))
                nc.gpsimd.tensor_scalar(hi.bitcast(fp32r), piece, 1.0, 1.0, ALU.mult, ALU.mult).then_inc(s_qhi, 1)
                pool.wait_ge(s_qhi, k + 1)
                nc.gpsimd.tensor_tensor(piece.bitcast(fp32r), piece, hi, ALU.subtract).then_inc(s_qlo, 1)

            def load_y_parts(m):
                if m == LAST - 2:
                    pool.wait_ge(s_qst, 16 * QUARTERS)
                else:
                    for slot in range(2):
                        pool.wait_ge(s_jst[slot], 16 * (m + 1 + DC))
                if m % 2 == 0:
                    flat = stacks[:, 0, :, :, :].rearrange("p h s n -> p (h s) n")
                    pool.dma_start(flat[:, m:m + 2, :], y_split_dram[m]).then_inc(s_ypl[m], 16)
                elif m < 4:
                    hi, lo = y_parts(m)
                    pool.dma_start(lo, y_split_dram[m, :, 0, :]).then_inc(s_ypl[m], 16)
                    pool.dma_start(hi, y_split_dram[m, :, 1, :]).then_inc(s_ypl[m], 16)
                else:
                    pool.dma_start(stacks[:, 1, 0, 0:2, :], y_split_dram[m]).then_inc(s_ypl[m], 16)

            def load_wo(kind, half):
                rows = slice(kind * DC // 2, (kind + 1) * DC // 2)
                cols = slice(half * HALF, (half + 1) * HALF)
                pool.dma_start(h_lo[:, rows, cols], w_split_dram[half, 0, :, rows, :]).then_inc(s_wol[2 * kind + half], 16)
                pool.dma_start(h_hi[:, rows, cols], w_split_dram[half, 1, :, rows, :]).then_inc(s_wol[2 * kind + half], 16)

            split_w(0)
            split_w(1)
            for n in range(2 * DC):
                pool.wait_ge(s_hf, n + 1)
                th, d = n // DC, n % DC
                cols = slice(th * HALF, (th + 1) * HALF)
                nc.gpsimd.tensor_tensor(h_lo[:, d, cols], CUM[1][:, (n % 2) * HALF:(n % 2 + 1) * HALF],
                                        h_hi[:, d, cols].bitcast(fp32), ALU.subtract).then_inc(s_hlo, 1)
            split_w(2)
            split_w(3)

            def sb_probs(g):
                n = (g % TB + 1) * P
                pool.wait_ge(s_scan, SB_UNIT[g])
                nc.gpsimd.tensor_tensor(U[g % 2][:, 0:n - 1], U[g % 2][:, 0:n - 1], R[g % 2][:, 1:n],
                                        ALU.mult).then_inc(s_prob, 1)

            def fx_probs(g):
                n = (g % TB + 1) * P
                pool.wait_ge(s_inv, FX_UNIT[g])
                nc.gpsimd.tensor_scalar(U[g % 2][:, 0:n], U[g % 2][:, 0:n], row_inv[:, g % 2:g % 2 + 1], 1.0,
                                        ALU.mult, ALU.mult).then_inc(s_prob, 1)

            def gate_pair(p):
                pool.wait_ge(s_pvd, (p + 1) * STEPS // 2)
                pool.wait_ge(s_plo, LO_UNITS[p, "g", 1])
                nc.gpsimd.tensor_tensor(G_T, G_T, O_T, ALU.mult).then_inc(s_y, 1)

            def square_pair(p):
                pool.wait_ge(s_t, T_ITEM["V", p + 1, 1])
                nc.gpsimd.tensor_tensor(VT, O_T, O_T, ALU.mult).then_inc(s_sq, 1)

            split_w(N_FIRST)
            sb_probs(0)
            sb_probs(1)
            for g in range(UNITS):
                p, i = g // STEPS, g % STEPS
                if g + 1 < UNITS and not is_sb(g + 1):
                    fx_probs(g + 1)
                if g + 2 < UNITS and is_sb(g + 2):
                    sb_probs(g + 2)
                if i == 0 and p >= 1:
                    gate_pair(p - 1)
                if i == 1 and p >= 1:
                    square_pair(p - 1)
                b = N_FIRST + 4 * p + i // 4 + 1
                if i % 4 == 0 and b < len(blocks):
                    split_w(b)
                before = (p, i - 1)
                if before in JOB_AT:
                    do_job(JOB_AT[before])
                if before in QUARTER_AT:
                    split_quarter(QUARTER_AT[before])
                if (p, i) == (LAST - 1, STEPS - 2):
                    pool.wait_ge(s_score, S_PIECE[LAST * STEPS - 1, 1])
                    load_y_parts(0)
                if (p, i) == (LAST - 1, STEPS - 1):
                    load_y_parts(2)
                    load_y_parts(4)
                if p == LAST:
                    if i == 1:
                        pool.wait_ge(s_score, S_PIECE[g + 1, 0])
                        load_wo(0, 0)
                    if i == 3:
                        pool.wait_ge(s_score, S_PIECE[g + 1, 0])
                        load_wo(0, 1)
                    if i == 6:
                        pool.wait_ge(s_proj, len(units))
                        load_y_parts(1)
                    if i == 7:
                        load_y_parts(3)
                    if i == 8:
                        load_wo(1, 0)
                    if i == 10:
                        load_wo(1, 1)
                    if i == 12:
                        pool.wait_ge(s_score, S_PIECE[LAST * STEPS + TB - 1, 1])
                        load_y_parts(5)
            pool.wait_ge(s_pvd, GROUPS)
            pool.wait_ge(s_t, T_ITEM["T", UNITS - 1, 1])
            nc.gpsimd.tensor_tensor(SQUARES, O_T, O_T, ALU.mult).then_inc(s_sq, 1)

        @block.scalar
        def _(act):
            act.dma_start(ident[:], identity).then_inc(s_id, 16)
            act.dma_start(b_ada_sb, b_ada_cols).then_inc(s_const, 16)
            act.dma_start(g_norm_sb, g_norm_cols).then_inc(s_const, 16)
            act.dma_start(g_grp_sb, g_grp_cols).then_inc(s_const, 16)
            act.dma_start(b_f_sb, b_f_col).then_inc(s_const, 16)
            act.wait_ge(s_c, 16)
            nc.scalar.activation(CUM[1], CUM[0], ACT.Sigmoid).then_inc(s_csig, 1)

            def x_squares(h):
                for t in range(4 * h, 4 * h + 4):
                    act.wait_ge(s_x[t % 4], 16 * (h + 1))
                    nc.scalar.activation(h_lo[:, t % 4 + 4, :] if h == 0 else pt_hi[:, 4 * (t % 2):4 * (t % 2) + 4, :],
                                         work[:, t % 4, :] if h == 0
                                         else work[:, t % 4, :].rearrange("p (a n) -> p a n", a=4), ACT.Square,
                                         accum_out=ss_x[:, t:t + 1]).then_inc(s_ssx, 1)
                    if h == 1 and t < 6:
                        act.wait_ge(s_ssx, t + 1)
                act.wait_ge(s_rv, h + 1)
                nc.scalar.activation(rms_s[:, 4 * h:4 * h + 4], rms_v[:, 4 * h:4 * h + 4], ACT.Sqrt).then_inc(s_rs, 1)

            def h_piece(n):
                th, d = n // DC, n % DC
                act.wait_ge(s_xt, n + 1)
                nc.scalar.activation(h_hi[:, d, th * HALF:(th + 1) * HALF], psum[:, x_piece_bank(n), :],
                                     ACT.Identity, scale=a_cols[:, d:d + 1],
                                     bias=ada[:, d:d + 1]).then_inc(s_hhi, 1)

            def proj_out(u, first=True, second=True):
                p, kind, th = units[u]
                bank = PROJ[u % 2]
                st = p % 2
                cols = slice(th * HALF, (th + 1) * HALF)
                if first:
                    act.wait_ge(s_proj, u + 1)
                if kind == "k":
                    for a in range(2):
                        src = bank[a * HD:(a + 1) * HD, :]
                        if a == 0 and first or a == 1 and second:
                            nc.scalar.activation(stacks[0:HD, st, a, 1, cols], src, ACT.Copy)
                            nc.scalar.activation(stacks[HD:P, st, a, 1, cols], src,
                                                 ACT.Copy).then_inc(s_phi if a else s_phk, 1)
                    return
                if not first:
                    return
                if kind == "q":
                    nc.scalar.activation(stacks[0:HD, st, 0, 0, cols], bank[0:HD, :], ACT.Copy, scale=SCALE)
                    nc.scalar.activation(stacks[0:HD, st, 1, 0, cols], bank[HD:P, :], ACT.Copy,
                                         scale=SCALE).then_inc(s_phi, 1)
                elif kind == "v":
                    if p >= 2:
                        act.wait_ge(s_tfree, T_ITEM["SS", p - 2, 0])
                    nc.scalar.activation(VT[:, cols], bank, ACT.Copy).then_inc(s_phi, 1)
                elif kind == "g":
                    if p == LAST:
                        act.wait_ge(s_wlo, len(blocks))
                    elif p >= 1:
                        act.wait_ge(s_yst, 16 * p)
                    nc.scalar.activation(gate_of(p)[:, cols], bank, ACT.Sigmoid).then_inc(s_phi, 1)
                else:
                    nc.scalar.activation(CUM[1][0:8, cols], bank[0:8, :], ACT.Abs, bias=b_f_sb).then_inc(s_phi, 1)

            def scores_out(g):
                for j, (a, e) in enumerate(pieces(g)):
                    if is_sb(g):
                        if j == 0 and g % STEPS < 2 and JOBS_BY[g // STEPS - 1] > 0:
                            n = JOBS_BY[g // STEPS - 1]
                            act.wait_ge(s_jst[g % 2], 16 * len(range(g % 2, n, 2)))
                        if j == 0 and g >= 2:
                            act.wait_ge(s_t, T_ITEM["T", g - 2, len(tgroups(g - 2)) - 1])
                        act.wait_ge(s_score, S_PIECE[g, j])
                        bank = SCORE[(S_PIECE[g, j] - 1) % 3][:, 0:e - a]
                        nc.scalar.activation(U[g % 2][:, a:e], bank, ACT.Sigmoid)
                        nc.scalar.activation(R[g % 2][:, a:e], bank, ACT.Sigmoid, scale=-1.0).then_inc(s_sig, 1)
                if not is_sb(g):
                    n = (g % TB + 1) * P
                    act.wait_ge(s_max, FX_UNIT[g])
                    nc.scalar.activation(U[g % 2][:, 0:n], U[g % 2][:, 0:n], ACT.Exp, bias=neg_max[:, g % 2:g % 2 + 1],
                                         accum_out=row_sum[:, g % 2:g % 2 + 1]).then_inc(s_exp, 1)

            def values_out(q):
                a = (q // (TB // 2)) % 2
                act.wait_ge(s_pv, q + 1)
                if q >= 2:
                    act.wait_ge(s_pvd, q - 1)
                nc.scalar.activation(o_shift[a * HD:(a + 1) * HD, q % 2, :], OUT[HD:P, 0:2 * P],
                                     ACT.Copy).then_inc(s_pvs, 1)

            def vt_out(p, j):
                n = T_ITEM["V", p, j]
                act.wait_ge(s_t, n)
                bank = TRANS[(n - 1) % 2].rearrange("p (b d) -> p b d", d=P)
                for a in range(2):
                    last = nc.scalar.activation(v_stack[:, p % 2, a, 4 * j:4 * j + 4, 0:HD],
                                                bank[:, :, a * HD:(a + 1) * HD], ACT.Copy)
                last.then_inc(s_thi, 1)

            def pt_out(g):
                for j, (a, e) in enumerate(tgroups(g)):
                    n = T_ITEM["T", g, j]
                    act.wait_ge(s_t, n)
                    if j == 0 and g % 2 == 0 and g >= 2:
                        act.wait_ge(s_pv, g // 2)
                    bank = TRANS[(n - 1) % 2][:, 0:(e - a) * P].rearrange("p (b q) -> p b q", q=P)
                    nc.scalar.activation(pt_hi[:, a:e, (g % 2) * P:(g % 2 + 1) * P], bank,
                                         ACT.Copy).then_inc(s_thi, 1)

            def store(t):
                act.wait_ge(s_done, t + 1)
                act.dma_start(out_tiles[t], RES[t]).then_inc(s_store[t], 16)

            def final_square(t):
                act.wait_ge(s_fin, t + 1)
                nc.scalar.activation(pt_hi[:].rearrange("p a n -> p (a n)")[:, (t % 2) * D:(t % 2 + 1) * D], RES[t],
                                     ACT.Square, accum_out=ss_x[:, t:t + 1]).then_inc(s_fsq, 1)
                act.wait_ge(s_rv, 5 + t)
                nc.scalar.activation(row_sum[:, t % 2:t % 2 + 1], row_max[:, t % 2:t % 2 + 1],
                                     ACT.Sqrt).then_inc(s_rs, 1)

            x_squares(0)
            act.wait_ge(s_acol, 3)
            for n in range(DC):
                h_piece(n)
            x_squares(1)
            proj_out(0)
            for n in range(DC, DC + 6):
                h_piece(n)
            proj_out(1)
            for n in range(DC + 6, 2 * DC):
                h_piece(n)
            for u in range(2, 2 * N_FIRST):
                proj_out(u)
            act.wait_ge(s_phi, 2 * N_FIRST)
            nc.scalar.activation(CUM[1][0:8, :], CUM[1][0:8, :], ACT.Exp, scale=-1.0).then_inc(s_fa, 1)
            act.wait_ge(s_fa, 1)
            nc.scalar.activation(CUM[1][0:8, :], CUM[1][0:8, :], ACT.Ln, bias=1.0).then_inc(s_fa, 1)
            act.wait_ge(s_ada, 3 * DC)
            scores_out(0)
            scores_out(1)
            vt_out(0, 0)
            for g in range(UNITS):
                p, i = g // STEPS, g % STEPS
                u = 2 * N_FIRST + 8 * p + i // 2
                if p == LAST and i == squares_step(p) + 1:
                    act.wait_ge(s_rv, 3)
                    nc.scalar.activation(rms_s[:, 0:TB], rms_v[:, 0:TB], ACT.Sqrt).then_inc(s_rs, 1)
                if i == V_STEPS[0] and p + 1 < PAIRS:
                    vt_out(p + 1, 0)
                if i == V_STEPS[1]:
                    vt_out(p, 1)
                if g % 2 == 0 and g >= 2:
                    values_out(g // 2 - 1)
                pt_out(g)
                scores_first = g + 2 < UNITS and is_sb(g + 2)
                if scores_first:
                    scores_out(g + 2)
                if i % 2 == 1 and u < len(units):
                    proj_out(u, second=False)
                if i % 2 == 0 and 2 * N_FIRST < u < len(units) + 1:
                    proj_out(u - 1, first=False)
                if g + 2 < UNITS and not scores_first:
                    scores_out(g + 2)
            values_out(GROUPS - 1)
            act.wait_ge(s_rv, 4)
            nc.scalar.activation(rms_s[:, TB:2 * TB], rms_v[:, TB:2 * TB], ACT.Sqrt).then_inc(s_rs, 1)
            act.wait_ge(s_pv, GROUPS)
            for t in range(TB):
                final_square(t)
                if t >= 1:
                    store(t - 1)
            store(TB - 1)

        @block.vector
        def _(dve):
            refined = [0]

            def inverse_root(y, v, s, t, number):
                steps = refined[0]
                dve.wait_ge(s_rs, number)
                nc.vector.reciprocal(y, s).then_inc(s_rn, 1)
                dve.wait_ge(s_rn, steps + 1)
                nc.vector.tensor_tensor(t, y, y, ALU.mult).then_inc(s_rn, 1)
                dve.wait_ge(s_rn, steps + 2)
                nc.vector.tensor_tensor(t, t, v, ALU.mult).then_inc(s_rn, 1)
                dve.wait_ge(s_rn, steps + 3)
                nc.vector.tensor_scalar(t, t, -0.5, 1.5, ALU.mult, ALU.add).then_inc(s_rn, 1)
                dve.wait_ge(s_rn, steps + 4)
                nc.vector.tensor_tensor(y, y, t, ALU.mult).then_inc(s_rn, 1)
                dve.wait_ge(s_rn, steps + 5)
                refined[0] += 5

            def mean_square(v, ss, n):
                nc.vector.tensor_scalar(v, ss, 1.0 / n, EPS, ALU.mult, ALU.add).then_inc(s_rv, 1)

            def normalise_x(h):
                dve.wait_ge(s_ssx, 4 * h + 4)
                mean_square(rms_v[:, 4 * h:4 * h + 4], ss_x[:, 4 * h:4 * h + 4], D)
                dve.wait_ge(s_rv, h + 1)
                inverse_root(rms_y[:, 4 * h:4 * h + 4], rms_v[:, 4 * h:4 * h + 4], rms_s[:, 4 * h:4 * h + 4],
                             rms_t[:, 4 * h:4 * h + 4], h + 1)
                for t in range(4):
                    nc.vector.tensor_scalar(work[:, t, :], work[:, t, :], rms_y[:, 4 * h + t:4 * h + t + 1], None,
                                            ALU.mult).then_inc(s_xn, 1)

            nc.vector.memset(ones[:], 1.0).then_inc(s_ones, 1)
            nc.vector.memset(ss_o, 0.0).then_inc(s_ones, 1)
            dve.wait_ge(s_csig, 1)
            nc.vector.tensor_tensor(CUM[0], CUM[0], CUM[1], ALU.mult).then_inc(s_cact, 1)
            dve.wait_ge(s_cact, 1)

            def ada_column(n, stage, loaded, loads):
                dve.wait_ge(loaded, 16 * loads)
                junk = h_lo[:, n % 4, :] if n < 2 * DC else pt_lo[:, 4 * (n % 2):4 * (n % 2) + 4, :]
                if n >= 2 * DC:
                    stage = stage.rearrange("p (a n) -> p a n", a=4)
                c_act = CUM[0] if n < 2 * DC else CUM[0].rearrange("p (a n) -> p a n", a=4)
                if n >= 2:
                    dve.wait_ge(s_ada, n - 1)
                nc.vector.tensor_tensor_reduce(out=junk, in0=stage, in1=c_act, scale=1.0, scalar=0.0,
                                               op0=ALU.mult, op1=ALU.add,
                                               accum_out=ada[:, n:n + 1]).then_inc(s_ada, 1)

            for n in range(2 * DC):
                if n == 4:
                    normalise_x(0)
                ada_column(n, work[:, WA_SLOT[n % 4], :], s_wa[n % 4], n // 4 + 1)
            dve.wait_ge(s_const, 16 * 4)
            dve.wait_ge(s_ada, 2 * DC)
            nc.vector.tensor_tensor(ada[:, 0:2 * DC], ada[:, 0:2 * DC], b_ada_sb[:, 0:2 * DC],
                                    ALU.add).then_inc(s_acol, 1)
            dve.wait_ge(s_acol, 1)
            nc.vector.tensor_scalar(a_cols[:], ada[:, DC:2 * DC], 1.0, None, ALU.add).then_inc(s_acol, 1)
            dve.wait_ge(s_acol, 2)
            nc.vector.tensor_tensor(a_cols[:], a_cols[:], g_norm_sb, ALU.mult).then_inc(s_acol, 1)
            dve.wait_ge(s_acol, 3)

            def h_piece(n):
                dve.wait_ge(s_hhi, n + 1)
                if n >= 2:
                    dve.wait_ge(s_hlo, n - 1)
                d = n % DC
                nc.vector.tensor_scalar(CUM[1][:, (n % 2) * HALF:(n % 2 + 1) * HALF], psum[:, x_piece_bank(n), :],
                                        a_cols[:, d:d + 1], ada[:, d:d + 1], ALU.mult, ALU.add).then_inc(s_hf, 1)

            def proj_out(u, first=True, second=True):
                p, kind, th = units[u]
                bank = PROJ[u % 2]
                st = p % 2
                cols = slice(th * HALF, (th + 1) * HALF)
                if kind == "v":
                    return
                if kind == "k":
                    for a in range(2):
                        if a == 0 and first or a == 1 and second:
                            if a == 0:
                                dve.wait_ge(s_phk, k_units.index(u) + 1)
                            else:
                                dve.wait_ge(s_phi, u + 1)
                            for half in range(2):
                                last = nc.vector.tensor_tensor(
                                    stacks[half * HD:(half + 1) * HD, st, a, 2, cols], bank[a * HD:(a + 1) * HD, :],
                                    stacks[0:HD, st, a, 1, cols].bitcast(fp32), ALU.subtract)
                            if a == 1:
                                last.then_inc(s_plo, 1)
                    return
                if not first:
                    return
                dve.wait_ge(s_phi, u + 1)
                if kind == "q":
                    for a in range(2):
                        last = nc.vector.scalar_tensor_tensor(
                            out=stacks[HD:P, st, a, 0, cols], in0=bank[a * HD:(a + 1) * HD, :], scalar=SCALE,
                            in1=stacks[0:HD, st, a, 0, cols].bitcast(fp32), op0=ALU.mult, op1=ALU.subtract)
                    last.then_inc(s_plo, 1)
                elif kind == "g":
                    gate = gate_of(p)[:, cols]
                    nc.vector.scalar_tensor_tensor(out=gate, in0=bank, scalar=g_grp_sb[:, p_col(p):p_col(p) + 1],
                                                   in1=gate, op0=ALU.mult, op1=ALU.mult).then_inc(s_plo, 1)
                else:
                    if th == 0:
                        nc.vector.tensor_scalar(bf_neg, b_f_sb, -1.0, None, ALU.mult).then_inc(s_f, 1)
                        dve.wait_ge(s_f, 1)
                    nc.vector.tensor_scalar(G_T[0:8, cols], bank[0:8, :], -1.0, bf_neg, ALU.mult,
                                            ALU.add).then_inc(s_plo, 1)

            def p_col(p):
                return (p % 2) * (PAIRS // 2) + p // 2

            def scores_out(g):
                n = (g % TB + 1) * P
                if is_sb(g):
                    dve.wait_ge(s_sig, SB_PIECE[g, len(pieces(g)) - 1])
                    nc.vector.tensor_tensor_scan(R[g % 2][:, 0:n][:, ::-1], R[g % 2][:, 0:n][:, ::-1],
                                                 R[g % 2][:, 0:n][:, ::-1], 1.0, ALU.mult,
                                                 ALU.bypass).then_inc(s_scan, 1)
                    return
                k = FX_UNIT[g]
                slot = g % 2
                if g % TB == 0:
                    dve.wait_ge(s_cumb, 32 * (g // (2 * STEPS) + 1))
                dve.wait_ge(s_t, T_ITEM["T", g - 2, len(tgroups(g - 2)) - 1])
                if k > 2:
                    dve.wait_ge(s_max, k - 2)
                for j, (a, e) in enumerate(pieces(g)):
                    dve.wait_ge(s_score, S_PIECE[g, j])
                    nc.vector.tensor_tensor_reduce(
                        out=U[slot][:, a:e], in0=SCORE[(S_PIECE[g, j] - 1) % 3][:, 0:e - a],
                        in1=CUM[unit(g)[1]][:, a:e], scale=1.0, scalar=LOWEST, op0=ALU.add, op1=ALU.max,
                        accum_out=row_max[:, 2 * slot + j:2 * slot + j + 1]).then_inc(s_logit, 1)
                dve.wait_ge(s_logit, FX_PIECE[g, len(pieces(g)) - 1])
                nc.vector.tensor_reduce(neg_max[:, slot:slot + 1], row_max[:, 2 * slot:2 * slot + len(pieces(g))],
                                        op=ALU.max, axis=mybir.AxisListType.X, negate=True).then_inc(s_max, 1)

            def inverse_sum(g):
                dve.wait_ge(s_exp, FX_UNIT[g])
                nc.vector.reciprocal(row_inv[:, g % 2:g % 2 + 1], row_sum[:, g % 2:g % 2 + 1]).then_inc(s_inv, 1)

            def values_out(q):
                a = (q // (TB // 2)) % 2
                qb = (2 * q) % TB
                dve.wait_ge(s_pvs, q + 1)
                if q % (STEPS // 2) == 0 and q > 0:
                    dve.wait_ge(s_sq, q // (STEPS // 2))
                nc.vector.tensor_tensor(O_T[a * HD:(a + 1) * HD, qb * P:(qb + 2) * P], OUT[0:HD, 0:2 * P],
                                        o_shift[a * HD:(a + 1) * HD, q % 2, :], ALU.add).then_inc(s_pvd, 1)

            def vt_out(p, j):
                n = T_ITEM["V", p, j]
                dve.wait_ge(s_thi, T_HI["V", p, j])
                bank = TRANS[(n - 1) % 2].rearrange("p (b d) -> p b d", d=P)
                for a in range(2):
                    last = nc.vector.tensor_tensor(v_stack[:, p % 2, a, 4 * j:4 * j + 4, HD:P],
                                                   bank[:, :, a * HD:(a + 1) * HD],
                                                   v_stack[:, p % 2, a, 4 * j:4 * j + 4, 0:HD].bitcast(fp32),
                                                   ALU.subtract)
                last.then_inc(s_tfree, 1)

            def squares_out(p):
                n = T_ITEM["SS", p, 0]
                dve.wait_ge(s_t, n)
                if p >= 2:
                    dve.wait_ge(s_tfree, T_ITEM["SS", p - 2, 0])
                cols = slice((p % 2) * TB, (p % 2 + 1) * TB)
                nc.vector.tensor_tensor(ss_o[:, cols], TRANS[(n - 1) % 2][:, 0:TB], ss_o[:, cols],
                                        ALU.add).then_inc(s_tfree, 1)

            def pt_out(g):
                for j, (a, e) in enumerate(tgroups(g)):
                    n = T_ITEM["T", g, j]
                    dve.wait_ge(s_thi, T_HI["T", g, j])
                    bank = TRANS[(n - 1) % 2][:, 0:(e - a) * P].rearrange("p (b q) -> p b q", q=P)
                    q0 = (g % 2) * P
                    nc.vector.tensor_tensor(pt_lo[:, a:e, q0:q0 + P], bank, pt_hi[:, a:e, q0:q0 + P].bitcast(fp32),
                                            ALU.subtract).then_inc(s_tfree, 1)

            def sb_part_out(n):
                t, h = sb_units[n]
                k = sb_tiles.index(t)
                half = Z[k][:, h * HALF:(h + 1) * HALF]
                dve.wait_ge(s_opb, n + 1)
                dve.wait_ge(s_xr[k], 16)
                nc.vector.scalar_tensor_tensor(out=half, in0=PROJ[n % 2], scalar=rms_y[:, t:t + 1], in1=half,
                                               op0=ALU.mult, op1=ALU.add).then_inc(s_osb, 1)

            def split_y(m, source):
                hi, lo = y_parts(m)
                n = Y_SPLIT[m]
                nc.vector.tensor_copy(hi, source).then_inc(s_yhi, 1)
                dve.wait_ge(s_yhi, n)
                nc.vector.tensor_tensor(lo, source, hi.bitcast(fp32), ALU.subtract).then_inc(s_ylo, 1)

            for n in range(DC):
                h_piece(n)
            normalise_x(1)
            proj_out(0)
            for n in range(DC, DC + 6):
                h_piece(n)
            proj_out(1)
            for n in range(DC + 6, 2 * DC):
                h_piece(n)
            dve.wait_ge(s_id, 16)
            nc.vector.tensor_copy(ident_bf[:], ident[:]).then_inc(s_maskb, 1)
            dve.wait_ge(s_mask, 3)
            nc.vector.tensor_copy(mask_bf[:], mask_f[:]).then_inc(s_maskb, 1)
            for u in range(2, 2 * N_FIRST):
                if u < 2 + DC // 2:
                    for n in (2 * (u - 2), 2 * (u - 2) + 1):
                        ada_column(2 * DC + n, work[:, n % 4, :], s_wg[n % 4], n // 4 + 1)
                proj_out(u)
            dve.wait_ge(s_ada, 3 * DC)
            dve.wait_ge(s_hf, 2 * DC)
            nc.vector.scalar_tensor_tensor(out=a_cols[:], in0=ada[:, 2 * DC:3 * DC], scalar=1.0,
                                           in1=b_ada_sb[:, 2 * DC:3 * DC], op0=ALU.add,
                                           op1=ALU.add).then_inc(s_gate, 1)
            dve.wait_ge(s_plo, LO_UNITS[-1, "f", 1])
            nc.vector.tensor_scalar(G_T[0:8, :], G_T[0:8, :], 0.0, None, ALU.max).then_inc(s_f, 1)
            dve.wait_ge(s_f, 2)
            dve.wait_ge(s_fa, 2)
            nc.vector.tensor_tensor_scan(CUM[0][0:8, :], G_T[0:8, :], CUM[1][0:8, :], 0.0, ALU.add,
                                         ALU.add).then_inc(s_f, 2)
            scores_out(0)
            scores_out(1)
            vt_out(0, 0)
            for g in range(UNITS):
                p, i = g // STEPS, g % STEPS
                if g + 1 < UNITS and not is_sb(g + 1):
                    inverse_sum(g + 1)
                u = 2 * N_FIRST + 8 * p + i // 2
                if p == LAST and i > SB_FROM:
                    for n in range(SB_AT[i].start - (i == SB_FROM + 1), SB_AT[i].stop):
                        sb_part_out(n)
                if i == V_STEPS[0] and p + 1 < PAIRS:
                    vt_out(p + 1, 0)
                if i == V_STEPS[1]:
                    vt_out(p, 1)
                if g % 2 == 0 and g >= 2:
                    values_out(g // 2 - 1)
                if p >= 1 and i == squares_step(p):
                    squares_out(p - 1)
                    if p == LAST:
                        dve.wait_ge(s_tfree, T_ITEM["SS", LAST - 1, 0])
                        mean_square(rms_v[:, 0:TB], ss_o[:, 0:TB], N_TYPE)
                if p == LAST and i == squares_step(p) + 1:
                    inverse_root(rms_y[:, 0:TB], rms_v[:, 0:TB], rms_s[:, 0:TB], rms_t[:, 0:TB], 3)
                pt_out(g)
                if p == LAST and i == 1:
                    dve.wait_ge(s_y, LAST)
                    split_y(LAST - 1, G_T)
                if g + 2 < UNITS:
                    scores_out(g + 2)
                if i % 2 == 1 and u < len(units):
                    proj_out(u, second=False)
                if i % 2 == 0 and 2 * N_FIRST < u < len(units) + 1:
                    proj_out(u - 1, first=False)
            values_out(GROUPS - 1)

            dve.wait_ge(s_pvd, GROUPS)
            dve.wait_ge(s_plo, LO_UNITS[LAST, "g", 1])
            nc.vector.tensor_tensor(GATE_LAST, GATE_LAST, O_T, ALU.mult).then_inc(s_y, 1)
            dve.wait_ge(s_y, PAIRS)
            split_y(LAST, GATE_LAST)
            squares_out(LAST)
            dve.wait_ge(s_tfree, T_ITEM["SS", LAST, 0])
            mean_square(rms_v[:, TB:2 * TB], ss_o[:, TB:2 * TB], N_TYPE)
            dve.wait_ge(s_rv, 4)
            inverse_root(rms_y[:, TB:2 * TB], rms_v[:, TB:2 * TB], rms_s[:, TB:2 * TB], rms_t[:, TB:2 * TB], 4)

            def add_parts(t):
                dve.wait_ge(s_op, t + 1)
                if sb_tiles.index(t) < STORED:
                    dve.wait_ge(s_zld[sb_tiles.index(t)], 16)
                elif t == 0:
                    dve.wait_ge(s_osb, len(sb_units))
                tile = RES[t].rearrange("p (a n) -> p a n", a=2)
                nc.vector.scalar_tensor_tensor(out=tile, in0=psum[:, 2 * (t % 4):2 * (t % 4) + 2, :],
                                               scalar=rms_y[:, TB + t:TB + t + 1], in1=tile, op0=ALU.mult,
                                               op1=ALU.add).then_inc(s_fin, 1)

            def mean_of_tile(t):
                dve.wait_ge(s_fsq, t + 1)
                mean_square(row_max[:, t % 2:t % 2 + 1], ss_x[:, t:t + 1], D)

            def final_norm(t):
                slot = t % 2
                inverse_root(row_inv[:, slot:slot + 1], row_max[:, slot:slot + 1], row_sum[:, slot:slot + 1],
                             neg_max[:, slot:slot + 1], 5 + t)
                nc.vector.scalar_tensor_tensor(out=RES[t], in0=RES[t], scalar=row_inv[:, slot:slot + 1],
                                               in1=CUM[1], op0=ALU.mult, op1=ALU.mult).then_inc(s_done, 1)

            dve.wait_ge(s_row, 16)
            for t in range(TB + 1):
                if t >= 1:
                    mean_of_tile(t - 1)
                if t < TB:
                    add_parts(t)
                if t >= 1:
                    final_norm(t - 1)

        @block.tensor
        def _(pe):
            pe.wait_ge(s_id, 16)
            pe.wait_ge(s_xn, 4)

            def transpose_x(n):
                th, d = n // DC, n % DC
                if n >= 8:
                    pe.wait_ge(s_xn, 8)
                    pe.wait_ge(s_hf, n - 5)
                for t in range(4):
                    last = nc.tensor.transpose(psum[:, x_piece_bank(n), t * P:(t + 1) * P],
                                               work[:, t, d * P:(d + 1) * P], ident[:])
                last.then_inc(s_xt, 1)

            def proj(u, first, last_chunk):
                p, kind, th = units[u]
                b = block_no[p, kind]
                bank = PROJ[u % 2]
                cols = slice(th * HALF, (th + 1) * HALF)
                if first == 0:
                    pe.wait_ge(s_wlo, b + 1)
                    if u in (0, 2):
                        pe.wait_ge(s_hlo, (th + 1) * DC)
                    if u >= 2:
                        before = units[u - 2]
                        if before[1] == "v":
                            pe.wait_ge(s_phi, u - 1)
                        else:
                            pe.wait_ge(s_plo, LO_UNITS[before])
                for c_ in range(first, last_chunk):
                    hi = w_hi[:, w_slot(b), c_, :]
                    lo = w_lo[:, w_slot(b), c_, :]
                    nc.tensor.matmul(bank, hi, h_hi[:, c_, cols], start=(c_ == 0), stop=False)
                    nc.tensor.matmul(bank, hi, h_lo[:, c_, cols], start=False, stop=False)
                    last = nc.tensor.matmul(bank, lo, h_hi[:, c_, cols], start=False, stop=(c_ == DC - 1))
                if last_chunk == DC:
                    last.then_inc(s_proj, 1)

            def scores(g):
                p, a, qb = unit(g)
                q = stacks[:, p % 2, a, 0, qb * P:(qb + 1) * P]
                if g % STEPS == 0:
                    pe.wait_ge(s_plo, LO_UNITS[p, "k", 1])
                for j, (c0, c1) in enumerate(pieces(g)):
                    n = S_PIECE[g, j]
                    bank = SCORE[(n - 1) % 3]
                    if n > 3:
                        before = piece_list[n - 4]
                        if is_sb(before[0]):
                            pe.wait_ge(s_sig, SB_PIECE[before])
                        else:
                            pe.wait_ge(s_logit, FX_PIECE[before])
                    diagonal = c1 == (qb + 1) * P
                    nc.tensor.matmul(bank[:, 0:c1 - c0], q, stacks[:, p % 2, a, 1, c0:c1], start=True, stop=False)
                    last = nc.tensor.matmul(bank[:, 0:c1 - c0], q, stacks[:, p % 2, a, 2, c0:c1], start=False,
                                            stop=not diagonal)
                    if diagonal:
                        last = nc.tensor.matmul(bank[:, c1 - c0 - P:c1 - c0], ident_bf[:],
                                                mask_bf[:, 0 if is_sb(g) else 1, :], start=False, stop=True)
                    last.then_inc(s_score, 1)

            def next_bank(item):
                n = T_ITEM[item]
                if n > 2:
                    pe.wait_ge(s_tfree, n - 2)
                return TRANS[(n - 1) % 2]

            def transpose_v(p, j):
                pe.wait_ge(s_phi, unit_no[p, "v", j] + 1)
                bank = next_bank(("V", p, j))
                for k in range(4):
                    last = nc.tensor.transpose(bank[:, k * P:(k + 1) * P],
                                               VT[:, (4 * j + k) * P:(4 * j + k + 1) * P], ident[:])
                last.then_inc(s_t, 1)

            def transpose_probs(g):
                pe.wait_ge(s_prob, g + 1)
                for j, (a, e) in enumerate(tgroups(g)):
                    bank = next_bank(("T", g, j))
                    for k in range(a, e):
                        last = nc.tensor.transpose(bank[:, (k - a) * P:(k - a + 1) * P],
                                                   U[g % 2][:, k * P:(k + 1) * P], ident[:])
                    last.then_inc(s_t, 1)

            def sum_squares(p):
                pe.wait_ge(s_sq, p + 1)
                bank = next_bank(("SS", p, 0))
                squares = SQUARES if p == LAST else VT
                for t in range(TB):
                    last = nc.tensor.matmul(bank[:, t:t + 1], squares[:, t * P:(t + 1) * P], ones[:], start=True, stop=True)
                last.then_inc(s_t, 1)

            def values(q):
                p, a, qb = unit(2 * q)
                g = 2 * q + 1
                pe.wait_ge(s_tfree, T_ITEM["T", g, len(tgroups(g)) - 1])
                if q >= 1:
                    pe.wait_ge(s_pvd, q)
                for k in range(qb + 2):
                    c0 = 0 if k <= qb else P
                    for n, src in enumerate((pt_hi, pt_lo)):
                        last = nc.tensor.matmul(OUT[:, c0:2 * P], v_stack[:, p % 2, a, k, :], src[:, k, c0:2 * P],
                                                start=(k == 0 and n == 0), stop=(k == qb + 1 and n == 1))
                last.then_inc(s_pv, 1)

            def out_products(bank, kind, t, half, pairs):
                for j in pairs:
                    m = kind * (PAIRS // 2) + j
                    hi, lo = y_parts(2 * j + kind)
                    yh, yl = hi[:, t * P:(t + 1) * P], lo[:, t * P:(t + 1) * P]
                    cols = slice(half * HALF, (half + 1) * HALF)
                    for k, (y_, w_) in enumerate(((yh, h_hi), (yh, h_lo), (yl, h_hi))):
                        last = nc.tensor.matmul(psum[:, bank, :], y_, w_[:, m, cols], start=(j == 0 and k == 0),
                                                stop=(j == PAIRS // 2 - 1 and k == 2))
                return last

            def sb_part(n):
                t, half = sb_units[n]
                if n == 0:
                    pe.wait_ge(s_ylo, Y_SPLIT[LAST - 1])
                    for m in (0, 2, 4):
                        pe.wait_ge(s_ypl[m], 16)
                    pe.wait_ge(s_wol[0], 32)
                if n == 2:
                    pe.wait_ge(s_wol[1], 32)
                if n < 2:
                    pe.wait_ge(s_plo, LO_UNITS[LAST, "g", n])
                else:
                    pe.wait_ge(s_osb, n - 1)
                out_products(n % 2, 0, t, half, range(PAIRS // 2)).then_inc(s_opb, 1)

            def fx_part(t, pairs):
                if pairs[0] == 0:
                    if t == 0:
                        for m in (1, 3):
                            pe.wait_ge(s_ypl[m], 32)
                        pe.wait_ge(s_ypl[5], 16)
                        pe.wait_ge(s_wol[2], 32)
                        pe.wait_ge(s_wol[3], 32)
                        pe.wait_ge(s_osb, len(sb_units))
                    if t >= 4:
                        pe.wait_ge(s_fin, t - 3)
                if pairs[-1] == PAIRS // 2 - 1 and t == 0:
                    pe.wait_ge(s_ylo, Y_SPLIT[LAST])
                for half in range(2):
                    last = out_products(2 * (t % 4) + half, 1, t, half, pairs)
                if pairs[-1] == PAIRS // 2 - 1:
                    last.then_inc(s_op, 1)

            for n in range(DC):
                transpose_x(n)
            proj(0, 0, DC)
            for n in range(DC, DC + 6):
                transpose_x(n)
            proj(1, 0, DC)
            for n in range(DC + 6, 2 * DC):
                transpose_x(n)
            for u in range(2, 2 * N_FIRST):
                proj(u, 0, DC)
            pe.wait_ge(s_maskb, 2)
            scores(0)
            scores(1)
            transpose_v(0, 0)
            for g in range(UNITS):
                p, i = g // STEPS, g % STEPS
                u = 2 * N_FIRST + 8 * p + i // 2
                if u < len(units) and (p + 1 < PAIRS or i < 4):
                    proj(u, (i % 2) * DC // 2, (i % 2 + 1) * DC // 2)
                if p == LAST:
                    for n in SB_AT.get(i, ()):
                        sb_part(n)
                if i == V_STEPS[0] and p + 1 < PAIRS:
                    transpose_v(p + 1, 0)
                if i == V_STEPS[1]:
                    transpose_v(p, 1)
                if g + 2 < UNITS:
                    scores(g + 2)
                if g % 2 == 0 and g >= 2:
                    values(g // 2 - 1)
                if p >= 1 and i == squares_step(p):
                    sum_squares(p - 1)
                transpose_probs(g)
            values(GROUPS - 1)
            fx_part(0, range(PAIRS // 2 - 1))
            pe.wait_ge(s_logit, FX_PIECE[UNITS - 1, 1])
            fx_part(1, range(PAIRS // 2 - 1))
            sum_squares(LAST)
            for t in range(2):
                fx_part(t, [PAIRS // 2 - 1])
            pe.wait_ge(s_tfree, T_ITEM["SS", LAST, 0])
            for t in range(2, TB):
                fx_part(t, range(PAIRS // 2))


def kernel(x, c, w_ada, b_ada, g_norm, w_in, b_f, g_grp, w_out, g_final):
    import concourse.bacc as bacc
    from concourse.bass_utils import run_bass_kernel_spmd

    def columns(v):
        return np.ascontiguousarray(np.asarray(v).reshape(-1, 128).T)

    x = np.asarray(x)
    batch, seq, d = x.shape
    arrays = {
        "in_x": np.ascontiguousarray(x[0]),
        "in_c": np.ascontiguousarray(c),
        "in_w_ada_t": np.ascontiguousarray(np.asarray(w_ada)[0].T),
        "in_b_ada": columns(b_ada),
        "in_g_norm": columns(g_norm),
        "in_w_in": np.ascontiguousarray(np.asarray(w_in)[0]),
        "in_b_f": np.ascontiguousarray(np.asarray(b_f).reshape(-1, 1)),
        "in_g_grp": columns(g_grp),
        "in_w_out": np.ascontiguousarray(np.asarray(w_out)[0]),
        "in_g_final": np.ascontiguousarray(np.asarray(g_final).reshape(1, -1)),
        "in_identity": np.eye(128, dtype=np.float32),
    }
    nc = bacc.Bacc("TRN2", target_bir_lowering=False, num_devices=1)
    args = [nc.dram_tensor(n, a.shape, mybir.dt.from_np(a.dtype), kind="ExternalInput").ap()
            for n, a in arrays.items()]
    out = nc.dram_tensor("out_x", (seq, d), mybir.dt.float32, kind="ExternalOutput").ap()
    hybrid_trunk_kernel(nc, *args, out)
    got = run_bass_kernel_spmd(nc, [arrays], core_ids=[0])
    return got.results[0]["out_x"].reshape(batch, seq, d)
```

```python
from contextlib import ExitStack

import numpy as np

import concourse.bass as bass
from concourse import mybir


def hybrid_trunk_kernel(nc, x, c, w_ada_t, b_ada_cols, g_norm_cols, w_in, b_f_col, g_grp_cols, w_out, g_final,
                        identity, out):
    fp32 = mybir.dt.float32
    fp32r = mybir.dt.float32r
    bf16 = mybir.dt.bfloat16
    ALU = mybir.AluOpType
    ACT = mybir.ActivationFunctionType

    P = 128
    SEQ, D = x.shape
    HD = 64
    DC = D // P
    TB = SEQ // P
    HALF = 512
    NHALF = SEQ // HALF
    N_TYPE = 512
    PAIRS = 2 * N_TYPE // P
    STEPS = 2 * TB
    UNITS = PAIRS * STEPS
    GROUPS = UNITS // 2
    EPS = 1e-6
    MASKED = -1e30
    SCALE = HD ** -0.5
    LOWEST = -3e38

    def is_sb(g):
        return (g // STEPS) % 2 == 0

    def unit(g):
        return g // STEPS, (g % STEPS) // TB, g % TB

    def pieces(g):
        n = (g % TB + 1) * P
        return [(a, min(a + HALF, n)) for a in range(0, n, HALF)]

    def tgroups(g):
        n = g % TB + 1
        return [(a, min(a + 4, n)) for a in range(0, n, 4)]

    def numbered(events):
        return {e: i + 1 for i, e in enumerate(events)}

    blocks = [(0, "q"), (0, "k"), (0, "v"), (-1, "f")]
    for p in range(PAIRS):
        if p + 1 < PAIRS:
            blocks += [(p + 1, "q"), (p + 1, "k"), (p, "g"), (p + 1, "v")]
        else:
            blocks += [(p, "g")]
    N_FIRST = 4
    F_LO = 32
    units = [(p, kind, h) for h in range(NHALF) for p, kind in blocks[:N_FIRST]]
    units += [(p, kind, h) for p, kind in blocks[N_FIRST:] for h in range(NHALF)]
    block_no = {b: i for i, b in enumerate(blocks)}
    unit_no = {u: i for i, u in enumerate(units)}
    k_units = [i for i, u in enumerate(units) if u[1] == "k"]

    def w_columns(p, kind):
        t, j = p % 2, p // 2
        if kind == "f":
            return w_in[:, 8 * N_TYPE:8 * N_TYPE + 8], 8
        base = 6 * N_TYPE + t * N_TYPE if kind == "g" else (3 * t + "qkv".index(kind)) * N_TYPE
        return w_in[:, base + P * j:base + P * (j + 1)], P

    all_units = list(range(UNITS))
    S_PIECE = numbered([(g, j) for g in all_units for j in range(len(pieces(g)))])
    SB_PIECE = numbered([(g, j) for g in all_units if is_sb(g) for j in range(len(pieces(g)))])
    FX_PIECE = numbered([(g, j) for g in all_units if not is_sb(g) for j in range(len(pieces(g)))])
    SB_UNIT = numbered([g for g in all_units if is_sb(g)])
    FX_UNIT = numbered([g for g in all_units if not is_sb(g)])
    piece_list = list(S_PIECE)

    def squares_step(p):
        return 3 if p == PAIRS - 1 else 5

    FORGET_AT = 9
    V_STEPS = [STEPS - 2, 2]
    t_items = [("V", 0, 0)]
    for g in all_units + [UNITS]:
        p, i = g // STEPS, g % STEPS
        if g < UNITS and i == V_STEPS[0] and p + 1 < PAIRS:
            t_items.append(("V", p + 1, 0))
        if g < UNITS and i == V_STEPS[1]:
            t_items.append(("V", p, 1))
        if g == UNITS or p >= 1 and i == squares_step(p):
            t_items.append(("SS", p - 1, 0))
        if g < UNITS:
            t_items += [("T", g, j) for j in range(len(tgroups(g)))]
    T_ITEM = numbered(t_items)
    T_HI = numbered([e for e in t_items if e[0] != "SS"])
    LO_UNITS = numbered([u for u in units if u[1] != "v"])
    LAST = PAIRS - 1
    Y_SPLIT = numbered([LAST - 1, LAST])

    jobs = [("w", h, m) for h in range(NHALF) for m in range(DC)]
    jobs += [("y", h, m) for m in range(LAST - 2) for h in range(NHALF)]
    job_steps = [(p, i) for p in (1, 3) for i in (1, 2, 5, 6, 8, 9, 10, 12)]
    job_steps += [(LAST - 2, i) for i in (1, 2, 4, 5, 6, 8, 9, 10, 11, 12)]
    JOB_AT = dict(zip(job_steps, range(len(jobs))))
    JOBS_BY = {p: sum(q <= p for q, _ in job_steps) for p in range(-1, PAIRS)}

    QUARTERS = 4
    QUARTER_AT = {(LAST - 1, 3 + 3 * k): k for k in range(QUARTERS)}

    STORED = 3
    sb_tiles = [(t + TB - STORED) % TB for t in range(TB)]
    sb_units = [(sb_tiles[t], h) for t, h in ((0, 0), (1, 0), (0, 1), (1, 1))]
    sb_units += [(t, h) for t in sb_tiles[2:] for h in range(2)]
    SB_FROM = 5
    SB_AT = {i: range((i - SB_FROM) * len(sb_units) // (STEPS - SB_FROM),
                      (i - SB_FROM + 1) * len(sb_units) // (STEPS - SB_FROM)) for i in range(SB_FROM, STEPS)}
    SB_NO = numbered(sb_units)
    X_AT = {1: (0, 1, 2), 3: (3,), 6: (4,)}

    x_tiles = x.rearrange("(t p) d -> t p d", p=P)
    out_tiles = out.rearrange("(t p) d -> t p d", p=P)
    ada_tiles = w_ada_t.rearrange("(n p) k -> n p k", p=P)
    wo_tiles = w_out.rearrange("(m p) n -> m p n", p=P)

    ctx = ExitStack()
    with ctx:
        def sb(name, shape, dt=fp32):
            return ctx.enter_context(nc.sbuf_tensor(name, shape, dt))

        def sem(name):
            return ctx.enter_context(nc.semaphore(name))

        y_dram = nc.dram_tensor("y_scratch", (PAIRS, P, SEQ), fp32, kind="Internal").ap()
        y_split_dram = nc.dram_tensor("y_split_scratch", (PAIRS, P, 2, SEQ), fp32, kind="Internal").ap()
        w_split_dram = nc.dram_tensor("w_split_scratch", (NHALF, 2, P, DC, HALF), fp32, kind="Internal").ap()
        c_dram = nc.dram_tensor("forget_scratch", (8, SEQ), fp32, kind="Internal").ap()
        sb_dram = nc.dram_tensor("sb_out_scratch", (TB, P, D), fp32, kind="Internal").ap()
        gate_dram = nc.dram_tensor("gate_scratch", (1, D), fp32, kind="Internal").ap()

        h_hi = sb("h_hi", [P, DC, SEQ], fp32r)
        h_lo = sb("h_lo", [P, DC, SEQ], fp32r)
        w_raw = sb("w_raw", [P, DC, P])
        w_hi = sb("w_hi", [P, 2, DC, P], fp32r)
        w_lo = sb("w_lo", [P, 2, DC, P], fp32r)
        stacks = sb("stacks", [P, 2, 2, 3, SEQ], fp32r)
        v_stack = sb("v_stack", [P, 2, 2, TB, P], fp32r)
        pt_hi = sb("pt_hi", [P, TB, 2 * P], fp32r)
        pt_lo = sb("pt_lo", [P, TB, 2 * P], fp32r)
        work = sb("work", [P, 9, SEQ])
        U = [work[:, 0, :], work[:, 1, :]]
        R = [work[:, 2, :], work[:, 3, :]]
        CUM = [work[:, 4, :], work[:, 5, :]]
        VT = work[:, 6, :]
        O_T = work[:, 7, :]
        G_T = work[:, 8, :]
        spare = sb("spare", [P, 2, HALF])
        gate_half = spare[:, 0, :]
        o_shift = spare[:, 1, :].rearrange("p (s n) -> p s n", s=2)
        ident = sb("ident", [P, P])
        ident_bf = sb("ident_bf", [P, P], bf16)
        mask_f = sb("mask_f", [P, 2, P])
        mask_bf = sb("mask_bf", [P, 2, P], bf16)
        ones = sb("ones", [P, 1])
        small = sb("small", [P, 192])
        ada = small[:, 0:24]
        b_ada_sb = small[:, 24:48]
        g_norm_sb = small[:, 48:56]
        g_grp_sb = small[:, 56:64]
        a_cols = small[:, 64:72]
        ss_x = small[:, 72:80]
        rms_v = small[:, 80:96]
        rms_s = small[:, 96:112]
        rms_y = small[:, 112:128]
        rms_t = small[:, 128:144]
        ss_o = small[:, 144:160]
        b_f_sb = small[0:8, 160:161]
        row_max = small[:, 164:168]
        neg_max = small[:, 168:170]
        row_sum = small[:, 170:172]
        row_inv = small[:, 172:174]
        bf_neg = small[0:8, 174:175]
        ss_last = small[:, 175:176]

        psum = ctx.enter_context(nc.psum_tensor("psum", [P, 8, 512], fp32))
        PROJ = [psum[:, 0, :], psum[:, 1, :], psum[:, 2, :]]
        SCORE = [psum[:, 2, :], psum[:, 3, :], psum[:, 4, :]]
        TRANS = [psum[:, 5, :], psum[:, 6, :]]
        OUT = psum[:, 7, :]

        s_const = sem("s_const")
        s_x = [sem(f"s_x{i}") for i in range(4)]
        s_wa = [sem(f"s_wa{i}") for i in range(4)]
        s_c = sem("s_c")
        s_csig = sem("s_csig")
        s_cact = sem("s_cact")
        s_ada = sem("s_ada")
        s_b1 = sem("s_b1")
        s_acol = sem("s_acol")
        s_ssx = sem("s_ssx")
        s_rv = sem("s_rv")
        s_rs = sem("s_rs")
        s_rn = sem("s_rn")
        s_xn = sem("s_xn")
        s_xt = sem("s_xt")
        s_hhi = sem("s_hhi")
        s_hf = sem("s_hf")
        s_hlo = sem("s_hlo")
        s_mask = sem("s_mask")
        s_maskb = sem("s_maskb")
        s_ones = sem("s_ones")
        s_wraw = sem("s_wraw")
        s_whi = sem("s_whi")
        s_wlo = sem("s_wlo")
        s_proj = sem("s_proj")
        s_phk = sem("s_phk")
        s_phi = sem("s_phi")
        s_plo = sem("s_plo")
        s_f = sem("s_f")
        s_fa = sem("s_fa")
        s_cum = sem("s_cum")
        s_cumb = sem("s_cumb")
        s_score = sem("s_score")
        s_sig = sem("s_sig")
        s_scan = sem("s_scan")
        s_logit = sem("s_logit")
        s_max = sem("s_max")
        s_exp = sem("s_exp")
        s_inv = sem("s_inv")
        s_prob = sem("s_prob")
        s_t = sem("s_t")
        s_thi = sem("s_thi")
        s_tfree = sem("s_tfree")
        s_pv = sem("s_pv")
        s_pvs = sem("s_pvs")
        s_pvd = sem("s_pvd")
        s_y = sem("s_y")
        s_sq = sem("s_sq")
        s_yst = sem("s_yst")
        s_yhi = sem("s_yhi")
        s_ylo = sem("s_ylo")
        s_grow = sem("s_grow")
        s_jld = [sem(f"s_jld{i}") for i in range(2)]
        s_jsc = sem("s_jsc")
        s_jhi = sem("s_jhi")
        s_jlo = sem("s_jlo")
        s_qld = sem("s_qld")
        s_qhi = sem("s_qhi")
        s_qlo = sem("s_qlo")
        s_qst = sem("s_qst")
        s_jst = [sem(f"s_jst{i}") for i in range(2)]
        s_ypl = [sem(f"s_ypl{i}") for i in range(PAIRS - 2)]
        s_wol = [sem(f"s_wol{i}") for i in range(4)]
        s_zst = [sem(f"s_zst{i}") for i in range(STORED)]
        s_zld = [sem(f"s_zld{i}") for i in range(STORED)]
        s_wg = [sem(f"s_wg{i}") for i in range(4)]
        s_id = sem("s_id")
        s_gate = sem("s_gate")
        s_gst = sem("s_gst")
        s_row = sem("s_row")
        s_op = sem("s_op")
        s_opb = sem("s_opb")
        s_osb = sem("s_osb")
        s_oph = sem("s_oph")
        s_finh = sem("s_finh")
        s_fin = sem("s_fin")
        s_fsq = sem("s_fsq")
        s_done = sem("s_done")
        s_xr = [sem(f"s_xr{i}") for i in range(TB)]
        s_store = [sem(f"s_store{i}") for i in range(TB)]

        block = ctx.enter_context(nc.Block())

        def proj_bank(u):
            return u % 3 if u < 2 * N_FIRST else u % 2

        def x_piece_bank(n):
            return 3 + n % 5

        def w_parts(b):
            if b in (2, 3):
                flat = stacks[:, 1, :, :, :].rearrange("p h s (c n) -> p (h s) c n", n=P)
                return flat[:, 2 * (b - 2)], flat[:, 2 * (b - 2) + 1]
            return w_hi[:, b % 2], w_lo[:, b % 2]

        def ada_column_of(n):
            return n // 2 + DC * (n % 2) if n < 2 * DC else n

        def y_parts(m):
            kind, j = m % 2, m // 2
            if kind == 0 and j < 3:
                flat = stacks[:, 0, :, :, :].rearrange("p h s n -> p (h s) n")
                return flat[:, 2 * j + 1, :], flat[:, 2 * j, :]
            if kind == 0:
                flat = v_stack[:, 0, :, :, :].rearrange("p h b n -> p h (b n)")
                return flat[:, 0, :], flat[:, 1, :]
            if j < 2:
                return tuple(w[:, j].rearrange("p c n -> p (c n)") for w in (w_hi, w_lo))
            return stacks[:, 1, j - 2, 1, :], stacks[:, 1, j - 2, 0, :]

        w_flat = w_raw[:].rearrange("p c n -> p (c n)")
        GATE_LAST = w_flat
        Z = [G_T, R[0], R[1], VT, CUM[0], G_T, R[0], R[1]]
        RES = Z[STORED:] + [U[1], O_T, U[0]]
        SQUARES = U[0]

        def gate_of(p):
            return GATE_LAST if p == LAST else G_T
        WA_SLOT = [6, 7, 8, 5]

        @block.sync
        def _(sp):
            sp.dma_start(CUM[0], c[0:1, :].partition_broadcast(P)).then_inc(s_c, 16)

            def load_w(b):
                p, kind = blocks[b]
                src, n = w_columns(p, kind)
                if b >= 1:
                    sp.wait_ge(s_wlo, b)
                sp.dma_start(w_raw[:, :, 0:n], src.rearrange("(c p) n -> p c n", p=P)).then_inc(s_wraw, 16)

            load_w(0)
            for t in range(4):
                sp.dma_start(work[:, t, :], x_tiles[t]).then_inc(s_x[t], 16)
            load_w(1)
            for n in range(2 * DC):
                if n == 3:
                    sp.wait_ge(s_cact, 1)
                if n >= 4:
                    sp.wait_ge(s_ada, n - 3)
                sp.dma_start(work[:, WA_SLOT[n % 4], :], ada_tiles[ada_column_of(n)]).then_inc(s_wa[n % 4], 16)
                if n in (2, 9):
                    load_w(2 + n // 9)
            sp.wait_ge(s_xt, DC)
            for t in range(4):
                sp.dma_start(work[:, t, :], x_tiles[4 + t]).then_inc(s_x[t], 16)

            def load_gate(n):
                sp.dma_start(work[:, n % 4, :], ada_tiles[2 * DC + n]).then_inc(s_wg[n % 4], 16)

            sp.wait_ge(s_xt, 2 * DC)
            for n in range(4):
                load_gate(n)
            load_w(N_FIRST)
            for n in range(4, DC):
                sp.wait_ge(s_ada, 2 * DC + n - 3)
                load_gate(n)
            sp.wait_ge(s_gate, 1)
            sp.dma_start(gate_dram.rearrange("a (b p) -> p (a b)", p=P), a_cols,
                         allow_slow_non_contiguous=True).then_inc(s_gst, 16)
            def load_job(n):
                kind, half, m = jobs[n]
                cols = slice(half * HALF, (half + 1) * HALF)
                slot = n % 2
                if (n - 1) // DC != n // DC and kind == "w":
                    sp.wait_ge(s_gst, 16)
                    if n > 0:
                        sp.wait_ge(s_jlo, n)
                    sp.dma_start(gate_half, gate_dram[0:1, cols].partition_broadcast(P)).then_inc(s_grow, 16)
                p = job_steps[n][0]
                if n == JOBS_BY[p - 1]:
                    sp.wait_ge(s_prob, p * STEPS)
                if n >= 2:
                    sp.wait_ge(s_jst[slot], 16 * (n // 2))
                if kind == "y":
                    sp.wait_ge(s_yst, 16 * (m + 1))
                src = wo_tiles[m] if kind == "w" else y_dram[m]
                sp.dma_start(R[slot][:, 0:HALF], src[:, cols]).then_inc(s_jld[slot], 16)

            def store_job(n):
                kind, half, m = jobs[n]
                slot = n % 2
                sp.wait_ge(s_jlo, n + 1)
                dst = (w_split_dram[half, :, :, m, :].rearrange("s p n -> p s n") if kind == "w"
                       else y_split_dram[m, :, :, half * HALF:(half + 1) * HALF])
                sp.dma_start(dst, R[slot].rearrange("p (s n) -> p s n", s=2)).then_inc(s_jst[slot], 16)

            def quarter(k):
                width = SEQ // QUARTERS
                if k >= 1:
                    sp.wait_ge(s_qlo, k)
                    sp.dma_start(y_split_dram[LAST - 2, :, :, (k - 1) * width:k * width],
                                 gate_half.rearrange("p (s n) -> p s n", s=2)).then_inc(s_qst, 16)
                if k < QUARTERS:
                    if k == 0:
                        sp.wait_ge(s_jlo, 2 * DC)
                        sp.wait_ge(s_yst, 16 * (LAST - 1))
                    else:
                        sp.wait_ge(s_qst, 16 * k)
                    sp.dma_start(gate_half[:, 0:width],
                                 y_dram[LAST - 2, :, k * width:(k + 1) * width]).then_inc(s_qld, 16)

            def load_x_again(n):
                if n == 0:
                    sp.wait_ge(s_ylo, Y_SPLIT[LAST - 1])
                    for slot in range(2):
                        sp.wait_ge(s_jst[slot], 16 * len(range(slot, len(jobs), 2)))
                    sp.wait_ge(s_prob, LAST * STEPS)
                if n == 3:
                    sp.wait_ge(s_tfree, T_ITEM["SS", LAST - 1, 0])
                if n == 4:
                    sp.wait_ge(s_logit, FX_PIECE[LAST * STEPS + TB - 1, 1])
                if n >= 5:
                    sp.wait_ge(s_zst[n - 5], 16)
                sp.dma_start(Z[n], x_tiles[sb_tiles[n]]).then_inc(s_xr[n], 16)

            def store_z(n):
                sp.wait_ge(s_osb, SB_NO[sb_tiles[n], 1])
                sp.dma_start(sb_dram[n], Z[n]).then_inc(s_zst[n], 16)

            pending = []
            for g in range(UNITS):
                p, i = g // STEPS, g % STEPS
                b = N_FIRST + 4 * p + i // 4 + 1
                if i % 4 == 0 and b < len(blocks):
                    load_w(b)
                if (p, i) in JOB_AT:
                    if len(pending) == 2:
                        store_job(pending.pop(0))
                    load_job(JOB_AT[p, i])
                    pending.append(JOB_AT[p, i])
                elif pending:
                    store_job(pending.pop(0))
                if (p, i) in QUARTER_AT:
                    quarter(QUARTER_AT[p, i])
                if p == LAST:
                    if i == 0:
                        quarter(QUARTERS)
                    if i in X_AT:
                        for n in X_AT[i]:
                            load_x_again(n)
                    for n in SB_AT.get(i - 1, ()):
                        t, h = sb_units[n]
                        k = sb_tiles.index(t)
                        if h == 1 and k < STORED:
                            store_z(k)
                            load_x_again(k + 5)
                if i == 2 and 1 <= p < LAST:
                    sp.wait_ge(s_y, p)
                    sp.dma_start(y_dram[p - 1], G_T).then_inc(s_yst, 16)
                if g == FORGET_AT + 2:
                    sp.wait_ge(s_f, 4)
                    sp.dma_start(c_dram, CUM[0][0:8, :]).then_inc(s_cum, 16)
                    sp.wait_ge(s_cum, 16)
                if i == (3 if p else FORGET_AT + 2) and p % 2 == 0:
                    if p >= 2:
                        sp.wait_ge(s_logit, FX_PIECE[p * STEPS - 1, 1])
                    for a in range(2):
                        sp.dma_start(CUM[a], c_dram[p + a:p + a + 1, :].partition_broadcast(P)).then_inc(s_cumb, 16)

            def load_z(n):
                sp.wait_ge(s_zst[n], 16)
                sp.dma_start(RES[sb_tiles[n]], sb_dram[n]).then_inc(s_zld[n], 16)

            sp.wait_ge(s_logit, FX_PIECE[UNITS - 1, 1])
            sp.dma_start(CUM[1], g_final[0:1, :].partition_broadcast(P)).then_inc(s_row, 16)
            sp.wait_ge(s_t, T_ITEM["T", UNITS - 1, 1])
            load_z(0)
            sp.wait_ge(s_sq, PAIRS)
            sp.wait_ge(s_y, PAIRS)
            load_z(1)
            sp.wait_ge(s_t, T_ITEM["SS", LAST, 0])
            load_z(2)
            sp.wait_ge(s_done, TB)
            sp.dma_start(out_tiles[TB - 1][:, 0:HALF], RES[TB - 1][:, 0:HALF]).then_inc(s_store[TB - 1], 16)
            for t in range(TB):
                sp.wait_ge(s_store[t], 16 if t < TB - 1 else 32)

        @block.gpsimd
        def _(pool):
            nc.gpsimd.memset(mask_f[:], 0.0).then_inc(s_mask, 1)
            pool.wait_ge(s_mask, 1)
            nc.gpsimd.affine_select(out=mask_f[:, 0, :], in_=mask_f[:, 0, :], compare_op=ALU.is_gt, fill=MASKED,
                                    base=0, pattern=[[-1, P]], channel_multiplier=1).then_inc(s_mask, 1)
            nc.gpsimd.affine_select(out=mask_f[:, 1, :], in_=mask_f[:, 1, :], compare_op=ALU.is_ge, fill=MASKED,
                                    base=0, pattern=[[-1, P]], channel_multiplier=1).then_inc(s_mask, 1)

            def split_w(b):
                if b >= N_FIRST:
                    before = b - N_FIRST if b < N_FIRST + 2 else b - 2
                    pool.wait_ge(s_proj, unit_no[blocks[before] + (1,)] + 1)
                pool.wait_ge(s_wraw, 16 * (b + 1))
                hi, lo = w_parts(b)
                nc.gpsimd.tensor_scalar(hi, w_raw[:], 1.0, 1.0, ALU.mult, ALU.mult).then_inc(s_whi, 1)
                pool.wait_ge(s_whi, b + 1)
                if blocks[b][1] == "f":
                    nc.gpsimd.tensor_tensor(hi[:, :, F_LO:F_LO + 8], w_raw[:, :, 0:8], hi[:, :, 0:8].bitcast(fp32),
                                            ALU.subtract).then_inc(s_wlo, 1)
                    return
                nc.gpsimd.tensor_tensor(lo, w_raw[:], hi.bitcast(fp32), ALU.subtract).then_inc(s_wlo, 1)

            def do_job(n):
                kind, half, m = jobs[n]
                slot = n % 2
                piece, hi = R[slot][:, 0:HALF], R[slot][:, HALF:2 * HALF]
                pool.wait_ge(s_jld[slot], 16 * (n // 2 + 1))
                if kind == "w":
                    pool.wait_ge(s_grow, 16 * (half + 1))
                    nc.gpsimd.tensor_tensor(piece, piece, gate_half, ALU.mult).then_inc(s_jsc, 1)
                    pool.wait_ge(s_jsc, n + 1)
                nc.gpsimd.tensor_scalar(hi.bitcast(fp32r), piece, 1.0, 1.0, ALU.mult, ALU.mult).then_inc(s_jhi, 1)
                pool.wait_ge(s_jhi, n + 1)
                nc.gpsimd.tensor_tensor(piece.bitcast(fp32r), piece, hi, ALU.subtract).then_inc(s_jlo, 1)

            def split_quarter(k):
                width = SEQ // QUARTERS
                piece, hi = gate_half[:, 0:width], gate_half[:, width:2 * width]
                pool.wait_ge(s_qld, 16 * (k + 1))
                nc.gpsimd.tensor_scalar(hi.bitcast(fp32r), piece, 1.0, 1.0, ALU.mult, ALU.mult).then_inc(s_qhi, 1)
                pool.wait_ge(s_qhi, k + 1)
                nc.gpsimd.tensor_tensor(piece.bitcast(fp32r), piece, hi, ALU.subtract).then_inc(s_qlo, 1)

            def load_y_parts(m):
                if m == LAST - 2:
                    pool.wait_ge(s_qst, 16 * QUARTERS)
                else:
                    for slot in range(2):
                        pool.wait_ge(s_jst[slot], 16 * (m + 1 + DC))
                if m % 2 == 0:
                    flat = stacks[:, 0, :, :, :].rearrange("p h s n -> p (h s) n")
                    pool.dma_start(flat[:, m:m + 2, :], y_split_dram[m]).then_inc(s_ypl[m], 16)
                elif m < 4:
                    hi, lo = y_parts(m)
                    pool.dma_start(lo, y_split_dram[m, :, 0, :]).then_inc(s_ypl[m], 16)
                    pool.dma_start(hi, y_split_dram[m, :, 1, :]).then_inc(s_ypl[m], 16)
                else:
                    pool.dma_start(stacks[:, 1, 0, 0:2, :], y_split_dram[m]).then_inc(s_ypl[m], 16)

            def load_wo(kind, half):
                rows = slice(kind * DC // 2, (kind + 1) * DC // 2)
                cols = slice(half * HALF, (half + 1) * HALF)
                pool.dma_start(h_lo[:, rows, cols], w_split_dram[half, 0, :, rows, :]).then_inc(s_wol[2 * kind + half], 16)
                pool.dma_start(h_hi[:, rows, cols], w_split_dram[half, 1, :, rows, :]).then_inc(s_wol[2 * kind + half], 16)

            def h_lo_piece(n):
                pool.wait_ge(s_hf, n + 1)
                th, d = n // DC, n % DC
                cols = slice(th * HALF, (th + 1) * HALF)
                nc.gpsimd.tensor_tensor(h_lo[:, d, cols], spare[:, n % 2, :], h_hi[:, d, cols].bitcast(fp32),
                                        ALU.subtract).then_inc(s_hlo, 1)

            for b in range(3):
                split_w(b)
            for n in range(2 * DC):
                h_lo_piece(n)
                if n == DC - 1:
                    split_w(3)
                    pool.wait_ge(s_rn, 2 * 5)
                    nc.gpsimd.tensor_scalar(work[:, 2, :], work[:, 2, :], rms_y[:, 6:7], 1.0, ALU.mult,
                                            ALU.mult).then_inc(s_xn, 1)

            def sb_probs(g):
                n = (g % TB + 1) * P
                pool.wait_ge(s_scan, SB_UNIT[g])
                nc.gpsimd.tensor_tensor(U[g % 2][:, 0:n - 1], U[g % 2][:, 0:n - 1], R[g % 2][:, 1:n],
                                        ALU.mult).then_inc(s_prob, 1)

            def fx_probs(g):
                n = (g % TB + 1) * P
                pool.wait_ge(s_inv, FX_UNIT[g])
                nc.gpsimd.tensor_scalar(U[g % 2][:, 0:n], U[g % 2][:, 0:n], row_inv[:, g % 2:g % 2 + 1], 1.0,
                                        ALU.mult, ALU.mult).then_inc(s_prob, 1)

            def gate_pair(p):
                pool.wait_ge(s_pvd, (p + 1) * STEPS // 2)
                pool.wait_ge(s_plo, LO_UNITS[p, "g", 1])
                nc.gpsimd.tensor_tensor(G_T, G_T, O_T, ALU.mult).then_inc(s_y, 1)

            def square_pair(p):
                pool.wait_ge(s_t, T_ITEM["V", p + 1, 1])
                nc.gpsimd.tensor_tensor(VT, O_T, O_T, ALU.mult).then_inc(s_sq, 1)

            split_w(N_FIRST)
            sb_probs(0)
            sb_probs(1)
            for g in range(UNITS):
                p, i = g // STEPS, g % STEPS
                if g + 1 < UNITS and not is_sb(g + 1):
                    fx_probs(g + 1)
                if g + 2 < UNITS and is_sb(g + 2):
                    sb_probs(g + 2)
                if i == 0 and p >= 1:
                    gate_pair(p - 1)
                if i == 1 and p >= 1:
                    square_pair(p - 1)
                b = N_FIRST + 4 * p + i // 4 + 1
                if i % 4 == 0 and b < len(blocks):
                    split_w(b)
                before = (p, i - 1)
                if before in JOB_AT:
                    do_job(JOB_AT[before])
                if before in QUARTER_AT:
                    split_quarter(QUARTER_AT[before])
                if (p, i) == (LAST - 1, STEPS - 2):
                    pool.wait_ge(s_score, S_PIECE[LAST * STEPS - 1, 1])
                    load_y_parts(0)
                if (p, i) == (LAST - 1, STEPS - 1):
                    load_y_parts(2)
                    load_y_parts(4)
                if p == LAST:
                    if i == 1:
                        pool.wait_ge(s_score, S_PIECE[g + 1, 0])
                        load_wo(0, 0)
                    if i == 3:
                        pool.wait_ge(s_score, S_PIECE[g + 1, 0])
                        load_wo(0, 1)
                    if i == 6:
                        pool.wait_ge(s_proj, len(units))
                        load_y_parts(1)
                    if i == 7:
                        load_y_parts(3)
                    if i == 8:
                        load_wo(1, 0)
                    if i == 10:
                        load_wo(1, 1)
                    if i == 12:
                        pool.wait_ge(s_score, S_PIECE[LAST * STEPS + TB - 1, 1])
                        load_y_parts(5)
            pool.wait_ge(s_pvd, GROUPS)
            pool.wait_ge(s_t, T_ITEM["T", UNITS - 1, 1])
            nc.gpsimd.tensor_tensor(SQUARES, O_T, O_T, ALU.mult).then_inc(s_sq, 1)

        @block.scalar
        def _(act):
            act.dma_start(ident[:], identity).then_inc(s_id, 16)
            act.dma_start(b_ada_sb, b_ada_cols).then_inc(s_const, 16)
            act.dma_start(g_norm_sb, g_norm_cols).then_inc(s_const, 16)
            act.dma_start(g_grp_sb, g_grp_cols).then_inc(s_const, 16)
            act.dma_start(b_f_sb, b_f_col).then_inc(s_const, 16)
            act.wait_ge(s_c, 16)
            nc.scalar.activation(CUM[1], CUM[0], ACT.Sigmoid).then_inc(s_csig, 1)

            def x_squares(t):
                act.wait_ge(s_x[t % 4], 16 * (t // 4 + 1))
                if t >= 2:
                    act.wait_ge(s_ssx, t - 1)
                nc.scalar.activation(pt_hi[:, 4 * (t % 2):4 * (t % 2) + 4, :],
                                     work[:, t % 4, :].rearrange("p (a n) -> p a n", a=4), ACT.Square,
                                     accum_out=ss_x[:, t:t + 1]).then_inc(s_ssx, 1)

            def x_roots(h):
                act.wait_ge(s_rv, h + 1)
                nc.scalar.activation(rms_s[:, 4 * h:4 * h + 4], rms_v[:, 4 * h:4 * h + 4], ACT.Sqrt).then_inc(s_rs, 1)

            def h_piece(n):
                th, d = n // DC, n % DC
                act.wait_ge(s_xt, n + 1)
                act.wait_ge(s_acol, d + 1)
                nc.scalar.activation(h_hi[:, d, th * HALF:(th + 1) * HALF], psum[:, x_piece_bank(n), :],
                                     ACT.Identity, scale=a_cols[:, d:d + 1],
                                     bias=ada[:, d:d + 1]).then_inc(s_hhi, 1)
                if th == 0:
                    if n >= 2:
                        act.wait_ge(s_hlo, n - 1)
                    nc.scalar.activation(spare[:, n % 2, :], psum[:, x_piece_bank(n), :], ACT.Identity,
                                         scale=a_cols[:, d:d + 1], bias=ada[:, d:d + 1]).then_inc(s_hf, 1)

            def proj_out(u, first=True, second=True):
                p, kind, th = units[u]
                bank = PROJ[proj_bank(u)]
                st = p % 2
                cols = slice(th * HALF, (th + 1) * HALF)
                if first:
                    act.wait_ge(s_proj, u + 1)
                if kind == "k":
                    for a in range(2):
                        src = bank[a * HD:(a + 1) * HD, :]
                        if a == 0 and first or a == 1 and second:
                            nc.scalar.activation(stacks[0:HD, st, a, 1, cols], src, ACT.Copy)
                            nc.scalar.activation(stacks[HD:P, st, a, 1, cols], src,
                                                 ACT.Copy).then_inc(s_phi if a else s_phk, 1)
                    return
                if not first:
                    return
                if kind == "q":
                    nc.scalar.activation(stacks[0:HD, st, 0, 0, cols], bank[0:HD, :], ACT.Copy, scale=SCALE)
                    nc.scalar.activation(stacks[0:HD, st, 1, 0, cols], bank[HD:P, :], ACT.Copy,
                                         scale=SCALE).then_inc(s_phi, 1)
                elif kind == "v":
                    if p == 0:
                        act.wait_ge(s_ada, 2 * DC)
                    if p >= 2:
                        act.wait_ge(s_tfree, T_ITEM["SS", p - 2, 0])
                    nc.scalar.activation(VT[:, cols], bank, ACT.Copy).then_inc(s_phi, 1)
                elif kind == "g":
                    if p == LAST:
                        act.wait_ge(s_wlo, len(blocks))
                    elif p >= 1:
                        act.wait_ge(s_yst, 16 * p)
                    else:
                        act.wait_ge(s_f, 4)
                    nc.scalar.activation(gate_of(p)[:, cols], bank, ACT.Sigmoid).then_inc(s_phi, 1)
                else:
                    nc.scalar.activation(CUM[1][0:8, cols], bank[F_LO:F_LO + 8, :], ACT.Copy).then_inc(s_phi, 1)

            def scores_out(g):
                for j, (a, e) in enumerate(pieces(g)):
                    if is_sb(g):
                        if j == 0 and g % STEPS < 2 and JOBS_BY[g // STEPS - 1] > 0:
                            n = JOBS_BY[g // STEPS - 1]
                            act.wait_ge(s_jst[g % 2], 16 * len(range(g % 2, n, 2)))
                        if j == 0 and g >= 2:
                            act.wait_ge(s_t, T_ITEM["T", g - 2, len(tgroups(g - 2)) - 1])
                        act.wait_ge(s_score, S_PIECE[g, j])
                        bank = SCORE[(S_PIECE[g, j] - 1) % 3][:, 0:e - a]
                        nc.scalar.activation(U[g % 2][:, a:e], bank, ACT.Sigmoid)
                        nc.scalar.activation(R[g % 2][:, a:e], bank, ACT.Sigmoid, scale=-1.0).then_inc(s_sig, 1)
                if not is_sb(g):
                    n = (g % TB + 1) * P
                    act.wait_ge(s_max, FX_UNIT[g])
                    nc.scalar.activation(U[g % 2][:, 0:n], U[g % 2][:, 0:n], ACT.Exp, bias=neg_max[:, g % 2:g % 2 + 1],
                                         accum_out=row_sum[:, g % 2:g % 2 + 1]).then_inc(s_exp, 1)

            def values_out(q):
                a = (q // (TB // 2)) % 2
                act.wait_ge(s_pv, q + 1)
                if q >= 2:
                    act.wait_ge(s_pvd, q - 1)
                nc.scalar.activation(o_shift[a * HD:(a + 1) * HD, q % 2, :], OUT[HD:P, 0:2 * P],
                                     ACT.Copy).then_inc(s_pvs, 1)

            def vt_out(p, j):
                n = T_ITEM["V", p, j]
                act.wait_ge(s_t, n)
                bank = TRANS[(n - 1) % 2].rearrange("p (b d) -> p b d", d=P)
                for a in range(2):
                    last = nc.scalar.activation(v_stack[:, p % 2, a, 4 * j:4 * j + 4, 0:HD],
                                                bank[:, :, a * HD:(a + 1) * HD], ACT.Copy)
                last.then_inc(s_thi, 1)

            def pt_out(g):
                for j, (a, e) in enumerate(tgroups(g)):
                    n = T_ITEM["T", g, j]
                    act.wait_ge(s_t, n)
                    if j == 0 and g % 2 == 0 and g >= 2:
                        act.wait_ge(s_pv, g // 2)
                    bank = TRANS[(n - 1) % 2][:, 0:(e - a) * P].rearrange("p (b q) -> p b q", q=P)
                    nc.scalar.activation(pt_hi[:, a:e, (g % 2) * P:(g % 2 + 1) * P], bank,
                                         ACT.Copy).then_inc(s_thi, 1)

            def store(t):
                act.wait_ge(s_done, t + 1)
                act.dma_start(out_tiles[t], RES[t]).then_inc(s_store[t], 16)

            def last_squares():
                assert D == 2 ** (2 * (D.bit_length() // 2))
                t = TB - 1
                for half, done, sums in ((0, s_finh, ss_x[:, t:t + 1]), (1, s_fin, ss_last)):
                    act.wait_ge(done, 1 if half == 0 else TB)
                    place = (t % 2) * D + half * HALF
                    nc.scalar.activation(pt_hi[:].rearrange("p a n -> p (a n)")[:, place:place + HALF],
                                         RES[t][:, half * HALF:(half + 1) * HALF], ACT.Square, scale=D ** -0.5,
                                         accum_out=sums).then_inc(s_fsq, 1)
                act.wait_ge(s_rv, 5 + t)
                nc.scalar.activation(row_sum[:, t % 2:t % 2 + 1], row_max[:, t % 2:t % 2 + 1],
                                     ACT.Sqrt).then_inc(s_rs, 1)

            def final_square(t):
                act.wait_ge(s_fin, t + 1)
                nc.scalar.activation(pt_hi[:].rearrange("p a n -> p (a n)")[:, (t % 2) * D:(t % 2 + 1) * D], RES[t],
                                     ACT.Square, accum_out=ss_x[:, t:t + 1]).then_inc(s_fsq, 1)
                act.wait_ge(s_rv, 5 + t)
                nc.scalar.activation(row_sum[:, t % 2:t % 2 + 1], row_max[:, t % 2:t % 2 + 1],
                                     ACT.Sqrt).then_inc(s_rs, 1)

            for t in range(4):
                x_squares(t)
            x_roots(0)
            for n in range(DC):
                h_piece(n)
            for t in range(4, 8):
                x_squares(t)
            x_roots(1)
            proj_out(0)
            act.wait_ge(s_rn, 2 * 5)
            for t in range(2):
                nc.scalar.activation(work[:, t, :], work[:, t, :], ACT.Copy,
                                     scale=rms_y[:, 4 + t:5 + t]).then_inc(s_xn, 1)
            proj_out(1)
            proj_out(2)
            for n in range(DC, DC + 3):
                h_piece(n)
            proj_out(3)
            for n in range(DC + 3, 2 * DC):
                h_piece(n)
            for u in range(N_FIRST, 2 * N_FIRST):
                proj_out(u)
            def forget_sums():
                act.wait_ge(s_plo, LO_UNITS[-1, "f", 1])
                nc.scalar.activation(CUM[1][0:8, :], G_T[0:8, :], ACT.Abs, bias=b_f_sb).then_inc(s_fa, 1)
                act.wait_ge(s_fa, 1)
                nc.scalar.activation(CUM[1][0:8, :], CUM[1][0:8, :], ACT.Exp, scale=-1.0).then_inc(s_fa, 1)
                act.wait_ge(s_fa, 2)
                nc.scalar.activation(CUM[1][0:8, :], CUM[1][0:8, :], ACT.Ln, bias=1.0).then_inc(s_fa, 1)

            act.wait_ge(s_ada, 3 * DC)
            scores_out(0)
            scores_out(1)
            vt_out(0, 0)
            for g in range(UNITS):
                p, i = g // STEPS, g % STEPS
                u = 2 * N_FIRST + 8 * p + i // 2
                if p == LAST and i == squares_step(p) + 1:
                    act.wait_ge(s_rv, 3)
                    nc.scalar.activation(rms_s[:, 0:TB], rms_v[:, 0:TB], ACT.Sqrt).then_inc(s_rs, 1)
                if i == V_STEPS[0] and p + 1 < PAIRS:
                    vt_out(p + 1, 0)
                if i == V_STEPS[1]:
                    vt_out(p, 1)
                if g % 2 == 0 and g >= 2:
                    values_out(g // 2 - 1)
                pt_out(g)
                if g == FORGET_AT:
                    forget_sums()
                scores_first = g + 2 < UNITS and is_sb(g + 2)
                if scores_first:
                    scores_out(g + 2)
                if i % 2 == 1 and u < len(units):
                    proj_out(u, second=False)
                if i % 2 == 0 and 2 * N_FIRST < u < len(units) + 1:
                    proj_out(u - 1, first=False)
                if g + 2 < UNITS and not scores_first:
                    scores_out(g + 2)
            values_out(GROUPS - 1)
            act.wait_ge(s_rv, 4)
            nc.scalar.activation(rms_s[:, TB:2 * TB], rms_v[:, TB:2 * TB], ACT.Sqrt).then_inc(s_rs, 1)
            act.wait_ge(s_pv, GROUPS)
            for t in range(TB):
                if t < TB - 1:
                    final_square(t)
                else:
                    last_squares()
                if t >= 1:
                    store(t - 1)
            act.wait_ge(s_done, TB + 1)
            act.dma_start(out_tiles[TB - 1][:, HALF:], RES[TB - 1][:, HALF:]).then_inc(s_store[TB - 1], 16)

        @block.vector
        def _(dve):
            refined = [0]

            def inverse_root(y, v, s, t, number):
                steps = refined[0]
                dve.wait_ge(s_rs, number)
                nc.vector.reciprocal(y, s).then_inc(s_rn, 1)
                dve.wait_ge(s_rn, steps + 1)
                nc.vector.tensor_tensor(t, y, y, ALU.mult).then_inc(s_rn, 1)
                dve.wait_ge(s_rn, steps + 2)
                nc.vector.tensor_tensor(t, t, v, ALU.mult).then_inc(s_rn, 1)
                dve.wait_ge(s_rn, steps + 3)
                nc.vector.tensor_scalar(t, t, -0.5, 1.5, ALU.mult, ALU.add).then_inc(s_rn, 1)
                dve.wait_ge(s_rn, steps + 4)
                nc.vector.tensor_tensor(y, y, t, ALU.mult).then_inc(s_rn, 1)
                dve.wait_ge(s_rn, steps + 5)
                refined[0] += 5

            def mean_square(v, ss, n):
                nc.vector.tensor_scalar(v, ss, 1.0 / n, EPS, ALU.mult, ALU.add).then_inc(s_rv, 1)

            def x_roots(h):
                dve.wait_ge(s_ssx, 4 * h + 4)
                mean_square(rms_v[:, 4 * h:4 * h + 4], ss_x[:, 4 * h:4 * h + 4], D)
                dve.wait_ge(s_rv, h + 1)
                inverse_root(rms_y[:, 4 * h:4 * h + 4], rms_v[:, 4 * h:4 * h + 4], rms_s[:, 4 * h:4 * h + 4],
                             rms_t[:, 4 * h:4 * h + 4], h + 1)

            def normalise_x(h, tiles):
                for t in tiles:
                    nc.vector.tensor_scalar(work[:, t, :], work[:, t, :], rms_y[:, 4 * h + t:4 * h + t + 1], None,
                                            ALU.mult).then_inc(s_xn, 1)

            nc.vector.memset(ones[:], 1.0).then_inc(s_ones, 1)
            nc.vector.memset(ss_o, 0.0).then_inc(s_ones, 1)
            dve.wait_ge(s_csig, 1)
            nc.vector.tensor_tensor(CUM[0], CUM[0], CUM[1], ALU.mult).then_inc(s_cact, 1)
            dve.wait_ge(s_cact, 1)

            def ada_column(n, stage, loaded, loads):
                dve.wait_ge(loaded, 16 * loads)
                if n >= 2:
                    dve.wait_ge(s_ada, n - 1)
                col = ada_column_of(n)
                nc.vector.tensor_tensor_reduce(out=pt_lo[:, 4 * (n % 2):4 * (n % 2) + 4, :],
                                               in0=stage.rearrange("p (a n) -> p a n", a=4),
                                               in1=CUM[0].rearrange("p (a n) -> p a n", a=4), scale=1.0, scalar=0.0,
                                               op0=ALU.mult, op1=ALU.add,
                                               accum_out=ada[:, col:col + 1]).then_inc(s_ada, 1)

            def norm_columns(d):
                dve.wait_ge(s_ada, 2 * d + 2)
                nc.vector.tensor_tensor(ada[:, d:d + 1], ada[:, d:d + 1], b_ada_sb[:, d:d + 1], ALU.add)
                nc.vector.scalar_tensor_tensor(out=a_cols[:, d:d + 1], in0=ada[:, DC + d:DC + d + 1],
                                               scalar=b_ada_sb[:, DC + d:DC + d + 1], in1=g_norm_sb[:, d:d + 1],
                                               op0=ALU.add, op1=ALU.mult).then_inc(s_acol, 1)

            dve.wait_ge(s_const, 16 * 4)
            nc.vector.tensor_scalar(b_ada_sb[:, DC:2 * DC], b_ada_sb[:, DC:2 * DC], 1.0, None,
                                    ALU.add).then_inc(s_b1, 1)
            x_roots(0)
            dve.wait_ge(s_b1, 1)
            for n in range(2 * DC):
                if n == 2:
                    normalise_x(0, range(4))
                ada_column(n, work[:, WA_SLOT[n % 4], :], s_wa[n % 4], n // 4 + 1)
                if n >= 2 and n % 2 == 0:
                    norm_columns(n // 2 - 1)
            norm_columns(DC - 1)

            def h_piece(n):
                dve.wait_ge(s_hhi, n + 1)
                if n >= 2:
                    dve.wait_ge(s_hlo, n - 1)
                d = n % DC
                nc.vector.tensor_scalar(spare[:, n % 2, :], psum[:, x_piece_bank(n), :],
                                        a_cols[:, d:d + 1], ada[:, d:d + 1], ALU.mult, ALU.add).then_inc(s_hf, 1)

            def proj_out(u, first=True, second=True):
                p, kind, th = units[u]
                bank = PROJ[proj_bank(u)]
                st = p % 2
                cols = slice(th * HALF, (th + 1) * HALF)
                if kind == "v":
                    return
                if kind == "k":
                    for a in range(2):
                        if a == 0 and first or a == 1 and second:
                            if a == 0:
                                dve.wait_ge(s_phk, k_units.index(u) + 1)
                            else:
                                dve.wait_ge(s_phi, u + 1)
                            for half in range(2):
                                last = nc.vector.tensor_tensor(
                                    stacks[half * HD:(half + 1) * HD, st, a, 2, cols], bank[a * HD:(a + 1) * HD, :],
                                    stacks[0:HD, st, a, 1, cols].bitcast(fp32), ALU.subtract)
                            if a == 1:
                                last.then_inc(s_plo, 1)
                    return
                if not first:
                    return
                dve.wait_ge(s_phi, u + 1)
                if kind == "q":
                    for a in range(2):
                        last = nc.vector.scalar_tensor_tensor(
                            out=stacks[HD:P, st, a, 0, cols], in0=bank[a * HD:(a + 1) * HD, :], scalar=SCALE,
                            in1=stacks[0:HD, st, a, 0, cols].bitcast(fp32), op0=ALU.mult, op1=ALU.subtract)
                    last.then_inc(s_plo, 1)
                elif kind == "g":
                    gate = gate_of(p)[:, cols]
                    nc.vector.scalar_tensor_tensor(out=gate, in0=bank, scalar=g_grp_sb[:, p_col(p):p_col(p) + 1],
                                                   in1=gate, op0=ALU.mult, op1=ALU.mult).then_inc(s_plo, 1)
                else:
                    nc.vector.tensor_tensor(G_T[0:8, cols], bank[0:8, :], CUM[1][0:8, cols],
                                            ALU.add).then_inc(s_plo, 1)

            def p_col(p):
                return (p % 2) * (PAIRS // 2) + p // 2

            def scores_out(g):
                n = (g % TB + 1) * P
                if is_sb(g):
                    dve.wait_ge(s_sig, SB_PIECE[g, len(pieces(g)) - 1])
                    nc.vector.tensor_tensor_scan(R[g % 2][:, 0:n][:, ::-1], R[g % 2][:, 0:n][:, ::-1],
                                                 R[g % 2][:, 0:n][:, ::-1], 1.0, ALU.mult,
                                                 ALU.bypass).then_inc(s_scan, 1)
                    return
                k = FX_UNIT[g]
                slot = g % 2
                if g % TB == 0:
                    dve.wait_ge(s_cumb, 32 * (g // (2 * STEPS) + 1))
                dve.wait_ge(s_t, T_ITEM["T", g - 2, len(tgroups(g - 2)) - 1])
                if k > 2:
                    dve.wait_ge(s_max, k - 2)
                for j, (a, e) in enumerate(pieces(g)):
                    dve.wait_ge(s_score, S_PIECE[g, j])
                    nc.vector.tensor_tensor_reduce(
                        out=U[slot][:, a:e], in0=SCORE[(S_PIECE[g, j] - 1) % 3][:, 0:e - a],
                        in1=CUM[unit(g)[1]][:, a:e], scale=1.0, scalar=LOWEST, op0=ALU.add, op1=ALU.max,
                        accum_out=row_max[:, 2 * slot + j:2 * slot + j + 1]).then_inc(s_logit, 1)
                dve.wait_ge(s_logit, FX_PIECE[g, len(pieces(g)) - 1])
                nc.vector.tensor_reduce(neg_max[:, slot:slot + 1], row_max[:, 2 * slot:2 * slot + len(pieces(g))],
                                        op=ALU.max, axis=mybir.AxisListType.X, negate=True).then_inc(s_max, 1)

            def inverse_sum(g):
                dve.wait_ge(s_exp, FX_UNIT[g])
                nc.vector.reciprocal(row_inv[:, g % 2:g % 2 + 1], row_sum[:, g % 2:g % 2 + 1]).then_inc(s_inv, 1)

            def values_out(q):
                a = (q // (TB // 2)) % 2
                qb = (2 * q) % TB
                dve.wait_ge(s_pvs, q + 1)
                if q % (STEPS // 2) == 0 and q > 0:
                    dve.wait_ge(s_sq, q // (STEPS // 2))
                nc.vector.tensor_tensor(O_T[a * HD:(a + 1) * HD, qb * P:(qb + 2) * P], OUT[0:HD, 0:2 * P],
                                        o_shift[a * HD:(a + 1) * HD, q % 2, :], ALU.add).then_inc(s_pvd, 1)

            def vt_out(p, j):
                n = T_ITEM["V", p, j]
                dve.wait_ge(s_thi, T_HI["V", p, j])
                bank = TRANS[(n - 1) % 2].rearrange("p (b d) -> p b d", d=P)
                for a in range(2):
                    last = nc.vector.tensor_tensor(v_stack[:, p % 2, a, 4 * j:4 * j + 4, HD:P],
                                                   bank[:, :, a * HD:(a + 1) * HD],
                                                   v_stack[:, p % 2, a, 4 * j:4 * j + 4, 0:HD].bitcast(fp32),
                                                   ALU.subtract)
                last.then_inc(s_tfree, 1)

            def squares_out(p):
                n = T_ITEM["SS", p, 0]
                dve.wait_ge(s_t, n)
                if p >= 2:
                    dve.wait_ge(s_tfree, T_ITEM["SS", p - 2, 0])
                cols = slice((p % 2) * TB, (p % 2 + 1) * TB)
                nc.vector.tensor_tensor(ss_o[:, cols], TRANS[(n - 1) % 2][:, 0:TB], ss_o[:, cols],
                                        ALU.add).then_inc(s_tfree, 1)

            def pt_out(g):
                for j, (a, e) in enumerate(tgroups(g)):
                    n = T_ITEM["T", g, j]
                    dve.wait_ge(s_thi, T_HI["T", g, j])
                    bank = TRANS[(n - 1) % 2][:, 0:(e - a) * P].rearrange("p (b q) -> p b q", q=P)
                    q0 = (g % 2) * P
                    nc.vector.tensor_tensor(pt_lo[:, a:e, q0:q0 + P], bank, pt_hi[:, a:e, q0:q0 + P].bitcast(fp32),
                                            ALU.subtract).then_inc(s_tfree, 1)

            def sb_part_out(n):
                t, h = sb_units[n]
                k = sb_tiles.index(t)
                half = Z[k][:, h * HALF:(h + 1) * HALF]
                dve.wait_ge(s_opb, n + 1)
                dve.wait_ge(s_xr[k], 16)
                nc.vector.scalar_tensor_tensor(out=half, in0=PROJ[n % 2], scalar=rms_y[:, t:t + 1], in1=half,
                                               op0=ALU.mult, op1=ALU.add).then_inc(s_osb, 1)

            def forget_sums():
                nc.vector.tensor_scalar(bf_neg, b_f_sb, -1.0, None, ALU.mult).then_inc(s_f, 1)
                dve.wait_ge(s_f, 1)
                dve.wait_ge(s_fa, 1)
                nc.vector.tensor_scalar(G_T[0:8, :], G_T[0:8, :], -1.0, bf_neg, ALU.mult, ALU.add).then_inc(s_f, 1)
                dve.wait_ge(s_f, 2)
                nc.vector.tensor_scalar(G_T[0:8, :], G_T[0:8, :], 0.0, None, ALU.max).then_inc(s_f, 1)
                dve.wait_ge(s_f, 3)
                dve.wait_ge(s_fa, 3)
                nc.vector.tensor_tensor_scan(CUM[0][0:8, :], G_T[0:8, :], CUM[1][0:8, :], 0.0, ALU.add,
                                             ALU.add).then_inc(s_f, 1)

            def split_y(m, source):
                hi, lo = y_parts(m)
                n = Y_SPLIT[m]
                nc.vector.tensor_copy(hi, source).then_inc(s_yhi, 1)
                dve.wait_ge(s_yhi, n)
                nc.vector.tensor_tensor(lo, source, hi.bitcast(fp32), ALU.subtract).then_inc(s_ylo, 1)

            x_roots(1)
            proj_out(0)
            normalise_x(1, [3])
            proj_out(1)
            dve.wait_ge(s_acol, DC)
            for n in range(DC, DC + 3):
                h_piece(n)
            proj_out(3)
            for n in range(DC + 3, 2 * DC):
                h_piece(n)
            dve.wait_ge(s_id, 16)
            nc.vector.tensor_copy(ident_bf[:], ident[:]).then_inc(s_maskb, 1)
            dve.wait_ge(s_mask, 3)
            nc.vector.tensor_copy(mask_bf[:], mask_f[:]).then_inc(s_maskb, 1)
            for n in range(DC):
                if n == 4:
                    proj_out(N_FIRST)
                    proj_out(N_FIRST + 1)
                ada_column(2 * DC + n, work[:, n % 4, :], s_wg[n % 4], n // 4 + 1)
            proj_out(2 * N_FIRST - 1)
            dve.wait_ge(s_ada, 3 * DC)
            dve.wait_ge(s_hf, 2 * DC)
            nc.vector.scalar_tensor_tensor(out=a_cols[:], in0=ada[:, 2 * DC:3 * DC], scalar=1.0,
                                           in1=b_ada_sb[:, 2 * DC:3 * DC], op0=ALU.add,
                                           op1=ALU.add).then_inc(s_gate, 1)
            scores_out(0)
            scores_out(1)
            vt_out(0, 0)
            for g in range(UNITS):
                p, i = g // STEPS, g % STEPS
                if g + 1 < UNITS and not is_sb(g + 1):
                    inverse_sum(g + 1)
                u = 2 * N_FIRST + 8 * p + i // 2
                if p == LAST and i > SB_FROM:
                    for n in range(SB_AT[i].start - (i == SB_FROM + 1), SB_AT[i].stop):
                        sb_part_out(n)
                if i == V_STEPS[0] and p + 1 < PAIRS:
                    vt_out(p + 1, 0)
                if i == V_STEPS[1]:
                    vt_out(p, 1)
                if g % 2 == 0 and g >= 2:
                    values_out(g // 2 - 1)
                if p >= 1 and i == squares_step(p):
                    squares_out(p - 1)
                    if p == LAST:
                        dve.wait_ge(s_tfree, T_ITEM["SS", LAST - 1, 0])
                        mean_square(rms_v[:, 0:TB], ss_o[:, 0:TB], N_TYPE)
                if p == LAST and i == squares_step(p) + 1:
                    inverse_root(rms_y[:, 0:TB], rms_v[:, 0:TB], rms_s[:, 0:TB], rms_t[:, 0:TB], 3)
                pt_out(g)
                if g == FORGET_AT:
                    forget_sums()
                if p == LAST and i == 1:
                    dve.wait_ge(s_y, LAST)
                    split_y(LAST - 1, G_T)
                if g + 2 < UNITS:
                    scores_out(g + 2)
                if i % 2 == 1 and u < len(units):
                    proj_out(u, second=False)
                if i % 2 == 0 and 2 * N_FIRST < u < len(units) + 1:
                    proj_out(u - 1, first=False)
            values_out(GROUPS - 1)

            dve.wait_ge(s_pvd, GROUPS)
            dve.wait_ge(s_plo, LO_UNITS[LAST, "g", 1])
            nc.vector.tensor_tensor(GATE_LAST, GATE_LAST, O_T, ALU.mult).then_inc(s_y, 1)
            dve.wait_ge(s_y, PAIRS)
            split_y(LAST, GATE_LAST)
            squares_out(LAST)
            dve.wait_ge(s_tfree, T_ITEM["SS", LAST, 0])
            mean_square(rms_v[:, TB:2 * TB], ss_o[:, TB:2 * TB], N_TYPE)
            dve.wait_ge(s_rv, 4)
            inverse_root(rms_y[:, TB:2 * TB], rms_v[:, TB:2 * TB], rms_s[:, TB:2 * TB], rms_t[:, TB:2 * TB], 4)

            def add_parts(t):
                if t < TB - 1:
                    dve.wait_ge(s_op, t + 1)
                if sb_tiles.index(t) < STORED:
                    dve.wait_ge(s_zld[sb_tiles.index(t)], 16)
                elif t == 0:
                    dve.wait_ge(s_osb, len(sb_units))
                tile = RES[t].rearrange("p (a n) -> p a n", a=2)
                if t == TB - 1:
                    for half, in_psum, done in ((0, s_oph, s_finh), (1, s_op, s_fin)):
                        dve.wait_ge(in_psum, 1 if half == 0 else TB)
                        nc.vector.scalar_tensor_tensor(out=tile[:, half, :], in0=psum[:, 2 * (t % 4) + half, :],
                                                       scalar=rms_y[:, TB + t:TB + t + 1], in1=tile[:, half, :],
                                                       op0=ALU.mult, op1=ALU.add).then_inc(done, 1)
                    return
                nc.vector.scalar_tensor_tensor(out=tile, in0=psum[:, 2 * (t % 4):2 * (t % 4) + 2, :],
                                               scalar=rms_y[:, TB + t:TB + t + 1], in1=tile, op0=ALU.mult,
                                               op1=ALU.add).then_inc(s_fin, 1)

            def mean_of_tile(t):
                if t == TB - 1:
                    dve.wait_ge(s_fsq, TB + 1)
                    nc.vector.scalar_tensor_tensor(out=row_max[:, t % 2:t % 2 + 1], in0=ss_x[:, t:t + 1], scalar=EPS,
                                                   in1=ss_last, op0=ALU.add, op1=ALU.add).then_inc(s_rv, 1)
                    return
                dve.wait_ge(s_fsq, t + 1)
                mean_square(row_max[:, t % 2:t % 2 + 1], ss_x[:, t:t + 1], D)

            def final_norm(t):
                slot = t % 2
                inverse_root(row_inv[:, slot:slot + 1], row_max[:, slot:slot + 1], row_sum[:, slot:slot + 1],
                             neg_max[:, slot:slot + 1], 5 + t)
                for cols in [slice(0, D)] if t < TB - 1 else [slice(0, HALF), slice(HALF, D)]:
                    nc.vector.scalar_tensor_tensor(out=RES[t][:, cols], in0=RES[t][:, cols],
                                                   scalar=row_inv[:, slot:slot + 1], in1=CUM[1][:, cols],
                                                   op0=ALU.mult, op1=ALU.mult).then_inc(s_done, 1)

            dve.wait_ge(s_row, 16)
            for t in range(TB + 1):
                if t >= 1:
                    mean_of_tile(t - 1)
                if t < TB:
                    add_parts(t)
                if t >= 1:
                    final_norm(t - 1)

        @block.tensor
        def _(pe):
            pe.wait_ge(s_id, 16)
            pe.wait_ge(s_xn, 4)

            def transpose_x(n):
                th, d = n // DC, n % DC
                if n == DC:
                    pe.wait_ge(s_xn, 8)
                if n >= 5:
                    pe.wait_ge(s_hf, n - 4)
                for t in range(4):
                    last = nc.tensor.transpose(psum[:, x_piece_bank(n), t * P:(t + 1) * P],
                                               work[:, t, d * P:(d + 1) * P], ident[:])
                last.then_inc(s_xt, 1)

            def proj(u, first, last_chunk):
                p, kind, th = units[u]
                b = block_no[p, kind]
                bank = PROJ[proj_bank(u)]
                cols = slice(th * HALF, (th + 1) * HALF)
                if first == 0:
                    pe.wait_ge(s_wlo, b + 1)
                    earlier = [v for v in range(u) if proj_bank(v) == proj_bank(u)]
                    if earlier:
                        before = units[earlier[-1]]
                        if before[1] == "v":
                            pe.wait_ge(s_phi, earlier[-1] + 1)
                        else:
                            pe.wait_ge(s_plo, LO_UNITS[before])
                for c_ in range(first, last_chunk):
                    if u in (0, N_FIRST):
                        pe.wait_ge(s_hlo, th * DC + c_ + 1)
                    hi, lo = (w[:, c_, :] for w in w_parts(b))
                    nc.tensor.matmul(bank, hi, h_hi[:, c_, cols], start=(c_ == 0), stop=False)
                    last = nc.tensor.matmul(bank, hi, h_lo[:, c_, cols], start=False,
                                            stop=(kind == "f" and c_ == DC - 1))
                    if kind == "f":
                        continue
                    last = nc.tensor.matmul(bank, lo, h_hi[:, c_, cols], start=False, stop=(c_ == DC - 1))
                if last_chunk == DC:
                    last.then_inc(s_proj, 1)

            def scores(g):
                p, a, qb = unit(g)
                q = stacks[:, p % 2, a, 0, qb * P:(qb + 1) * P]
                if g % STEPS == 0:
                    pe.wait_ge(s_plo, LO_UNITS[p, "k", 1])
                for j, (c0, c1) in enumerate(pieces(g)):
                    n = S_PIECE[g, j]
                    bank = SCORE[(n - 1) % 3]
                    if n > 3:
                        before = piece_list[n - 4]
                        if is_sb(before[0]):
                            pe.wait_ge(s_sig, SB_PIECE[before])
                        else:
                            pe.wait_ge(s_logit, FX_PIECE[before])
                    diagonal = c1 == (qb + 1) * P
                    nc.tensor.matmul(bank[:, 0:c1 - c0], q, stacks[:, p % 2, a, 1, c0:c1], start=True, stop=False)
                    last = nc.tensor.matmul(bank[:, 0:c1 - c0], q, stacks[:, p % 2, a, 2, c0:c1], start=False,
                                            stop=not diagonal)
                    if diagonal:
                        last = nc.tensor.matmul(bank[:, c1 - c0 - P:c1 - c0], ident_bf[:],
                                                mask_bf[:, 0 if is_sb(g) else 1, :], start=False, stop=True)
                    last.then_inc(s_score, 1)

            def next_bank(item):
                n = T_ITEM[item]
                if n > 2:
                    pe.wait_ge(s_tfree, n - 2)
                return TRANS[(n - 1) % 2]

            def transpose_v(p, j):
                pe.wait_ge(s_phi, unit_no[p, "v", j] + 1)
                bank = next_bank(("V", p, j))
                for k in range(4):
                    last = nc.tensor.transpose(bank[:, k * P:(k + 1) * P],
                                               VT[:, (4 * j + k) * P:(4 * j + k + 1) * P], ident[:])
                last.then_inc(s_t, 1)

            def transpose_probs(g):
                pe.wait_ge(s_prob, g + 1)
                for j, (a, e) in enumerate(tgroups(g)):
                    bank = next_bank(("T", g, j))
                    for k in range(a, e):
                        last = nc.tensor.transpose(bank[:, (k - a) * P:(k - a + 1) * P],
                                                   U[g % 2][:, k * P:(k + 1) * P], ident[:])
                    last.then_inc(s_t, 1)

            def sum_squares(p):
                pe.wait_ge(s_sq, p + 1)
                bank = next_bank(("SS", p, 0))
                squares = SQUARES if p == LAST else VT
                for t in range(TB):
                    last = nc.tensor.matmul(bank[:, t:t + 1], squares[:, t * P:(t + 1) * P], ones[:], start=True, stop=True)
                last.then_inc(s_t, 1)

            def values(q):
                p, a, qb = unit(2 * q)
                g = 2 * q + 1
                pe.wait_ge(s_tfree, T_ITEM["T", g, len(tgroups(g)) - 1])
                if q >= 1:
                    pe.wait_ge(s_pvd, q)
                for k in range(qb + 2):
                    c0 = 0 if k <= qb else P
                    for n, src in enumerate((pt_hi, pt_lo)):
                        last = nc.tensor.matmul(OUT[:, c0:2 * P], v_stack[:, p % 2, a, k, :], src[:, k, c0:2 * P],
                                                start=(k == 0 and n == 0), stop=(k == qb + 1 and n == 1))
                last.then_inc(s_pv, 1)

            def out_products(bank, kind, t, half, pairs):
                for j in pairs:
                    m = kind * (PAIRS // 2) + j
                    hi, lo = y_parts(2 * j + kind)
                    yh, yl = hi[:, t * P:(t + 1) * P], lo[:, t * P:(t + 1) * P]
                    cols = slice(half * HALF, (half + 1) * HALF)
                    for k, (y_, w_) in enumerate(((yh, h_hi), (yh, h_lo), (yl, h_hi))):
                        last = nc.tensor.matmul(psum[:, bank, :], y_, w_[:, m, cols], start=(j == 0 and k == 0),
                                                stop=(j == PAIRS // 2 - 1 and k == 2))
                return last

            def sb_part(n):
                t, half = sb_units[n]
                if n == 0:
                    pe.wait_ge(s_ylo, Y_SPLIT[LAST - 1])
                    for m in (0, 2, 4):
                        pe.wait_ge(s_ypl[m], 16)
                    pe.wait_ge(s_wol[0], 32)
                if n == 2:
                    pe.wait_ge(s_wol[1], 32)
                if n < 2:
                    pe.wait_ge(s_plo, LO_UNITS[LAST, "g", n])
                else:
                    pe.wait_ge(s_osb, n - 1)
                out_products(n % 2, 0, t, half, range(PAIRS // 2)).then_inc(s_opb, 1)

            def fx_part(t, pairs):
                if pairs[0] == 0:
                    if t == 0:
                        for m in (1, 3):
                            pe.wait_ge(s_ypl[m], 32)
                        pe.wait_ge(s_ypl[5], 16)
                        pe.wait_ge(s_wol[2], 32)
                        pe.wait_ge(s_wol[3], 32)
                        pe.wait_ge(s_osb, len(sb_units))
                    if t >= 4:
                        pe.wait_ge(s_fin, t - 3)
                if pairs[-1] == PAIRS // 2 - 1 and t == 0:
                    pe.wait_ge(s_ylo, Y_SPLIT[LAST])
                for half in range(2):
                    last = out_products(2 * (t % 4) + half, 1, t, half, pairs)
                    if t == TB - 1 and half == 0:
                        last.then_inc(s_oph, 1)
                if pairs[-1] == PAIRS // 2 - 1:
                    last.then_inc(s_op, 1)

            for n in range(5):
                transpose_x(n)
            for d in range(DC):
                for u in range(3):
                    proj(u, d, d + 1)
                if d + 5 < DC:
                    transpose_x(d + 5)
            proj(3, 0, DC // 2)
            for n in range(DC, DC + 3):
                transpose_x(n)
            proj(3, DC // 2, DC)
            for n in range(DC + 3, DC + 5):
                transpose_x(n)
            for d in range(DC):
                for u in range(N_FIRST, N_FIRST + 3):
                    proj(u, d, d + 1)
                if d + 5 < DC:
                    transpose_x(DC + d + 5)
            pe.wait_ge(s_maskb, 2)
            proj(N_FIRST + 3, 0, DC - 2)
            scores(0)
            scores(1)
            proj(N_FIRST + 3, DC - 2, DC)
            transpose_v(0, 0)
            for g in range(UNITS):
                p, i = g // STEPS, g % STEPS
                u = 2 * N_FIRST + 8 * p + i // 2
                if u < len(units) and (p + 1 < PAIRS or i < 4):
                    proj(u, (i % 2) * DC // 2, (i % 2 + 1) * DC // 2)
                if p == LAST:
                    for n in SB_AT.get(i, ()):
                        sb_part(n)
                if i == V_STEPS[0] and p + 1 < PAIRS:
                    transpose_v(p + 1, 0)
                if i == V_STEPS[1]:
                    transpose_v(p, 1)
                if g + 2 < UNITS:
                    scores(g + 2)
                if g % 2 == 0 and g >= 2:
                    values(g // 2 - 1)
                if p >= 1 and i == squares_step(p):
                    sum_squares(p - 1)
                transpose_probs(g)
            fx_part(0, range(PAIRS // 2 - 1))
            values(GROUPS - 1)
            pe.wait_ge(s_logit, FX_PIECE[UNITS - 1, 1])
            fx_part(1, range(PAIRS // 2 - 1))
            sum_squares(LAST)
            for t in range(2):
                fx_part(t, [PAIRS // 2 - 1])
            pe.wait_ge(s_tfree, T_ITEM["SS", LAST, 0])
            for t in range(2, TB):
                fx_part(t, range(PAIRS // 2))


def kernel(x, c, w_ada, b_ada, g_norm, w_in, b_f, g_grp, w_out, g_final):
    import concourse.bacc as bacc
    from concourse.bass_utils import run_bass_kernel_spmd

    def columns(v):
        return np.ascontiguousarray(np.asarray(v).reshape(-1, 128).T)

    x = np.asarray(x)
    batch, seq, d = x.shape
    arrays = {
        "in_x": np.ascontiguousarray(x[0]),
        "in_c": np.ascontiguousarray(c),
        "in_w_ada_t": np.ascontiguousarray(np.asarray(w_ada)[0].T),
        "in_b_ada": columns(b_ada),
        "in_g_norm": columns(g_norm),
        "in_w_in": np.ascontiguousarray(np.asarray(w_in)[0]),
        "in_b_f": np.ascontiguousarray(np.asarray(b_f).reshape(-1, 1)),
        "in_g_grp": columns(g_grp),
        "in_w_out": np.ascontiguousarray(np.asarray(w_out)[0]),
        "in_g_final": np.ascontiguousarray(np.asarray(g_final).reshape(1, -1)),
        "in_identity": np.eye(128, dtype=np.float32),
    }
    nc = bacc.Bacc("TRN2", target_bir_lowering=False, num_devices=1)
    args = [nc.dram_tensor(n, a.shape, mybir.dt.from_np(a.dtype), kind="ExternalInput").ap()
            for n, a in arrays.items()]
    out = nc.dram_tensor("out_x", (seq, d), mybir.dt.float32, kind="ExternalOutput").ap()
    hybrid_trunk_kernel(nc, *args, out)
    got = run_bass_kernel_spmd(nc, [arrays], core_ids=[0])
    return got.results[0]["out_x"].reshape(batch, seq, d)
```
